# Optimizing a Trainium2 kernel written in Bass

```python
import jax, jax.numpy as jnp
from jax import lax
import numpy as np

D_MODEL = 1024
BATCH = 1
SEQ = 512
DEPTH = 1
DEC_BATCH = 8
DEC_SEQ = 1
PAST_LEN = 4096
PAGE_SIZE = 128

D_A = D_MODEL
D_B = D_MODEL
GROUP = 128
CONV_A_W = 31
CONV_B_W = 3
CONV_F_W = 3
D_FF = 2816
D_IN = 2 * D_A + 3 * D_B + 2 * D_MODEL
RMS_EPS = 1e-6
LN_EPS = 1e-5

kernel_name = "hybrid_conformer_shortconv_convffn_step"

def _rmsnorm(x, g):
    xf = x.astype(jnp.float32)
    r = lax.rsqrt(jnp.mean(xf * xf, axis=-1, keepdims=True) + RMS_EPS)
    return (xf * r).astype(x.dtype) * g

def _layernorm(x, g, b):
    xf = x.astype(jnp.float32)
    mu = jnp.mean(xf, axis=-1, keepdims=True)
    var = jnp.mean(jnp.square(xf - mu), axis=-1, keepdims=True)
    return ((xf - mu) * lax.rsqrt(var + LN_EPS)).astype(x.dtype) * g + b

def _causal_dwconv(u, buf, w):
    width = w.shape[0]
    full = jnp.concatenate([buf.astype(u.dtype), u], axis=1)
    out = lax.conv_general_dilated(
        full, w[:, None, :].astype(u.dtype), window_strides=(1,), padding="VALID",
        dimension_numbers=("NWC", "WIO", "NWC"), feature_group_count=u.shape[-1])
    new_buf = full[:, full.shape[1] - (width - 1):]
    return out, new_buf

def _layer(x, buf_a, buf_b, buf_f, g_mix, w_in, conv_a_w, conv_a_b, ln_a_g, ln_a_b, w_a_out,
           conv_b_w, w_b_out, w_o, g_ffn, w_up, conv_f_w, w_down):
    h = _rmsnorm(x, g_mix)
    z = jnp.einsum("btd,de->bte", h, w_in)
    splits = np.cumsum([D_A, D_A, D_B, D_B, D_B, D_MODEL]).tolist()
    a_val, a_gate, b_B, b_C, b_x, g_A, g_B = jnp.split(z, splits, axis=-1)
    u = a_val * jax.nn.sigmoid(a_gate)
    v, new_a = _causal_dwconv(u, buf_a, conv_a_w)
    v = _layernorm(v + conv_a_b, ln_a_g, ln_a_b)
    y_a = jnp.einsum("btc,cd->btd", jax.nn.silu(v), w_a_out)
    q, new_b = _causal_dwconv(b_C * b_x, buf_b, conv_b_w)
    y_b = jnp.einsum("btc,cd->btd", b_B * q, w_b_out)
    merged = jax.nn.sigmoid(g_A) * y_a + jax.nn.sigmoid(g_B) * y_b
    x = x + jnp.einsum("btd,de->bte", merged, w_o)
    h2 = _rmsnorm(x, g_ffn)
    f = jnp.einsum("btd,df->btf", h2, w_up)
    f_gate, f_up = jnp.split(f, [D_FF], axis=-1)
    f_conv, new_f = _causal_dwconv(f_gate, buf_f, conv_f_w)
    x = x + jnp.einsum("btf,fd->btd", jax.nn.silu(f_conv) * f_up, w_down)
    return x, new_a, new_b, new_f

def _trunk(x, bufs_a, bufs_b, bufs_f, g_mix, w_in, conv_a_w, conv_a_b, ln_a_g, ln_a_b, w_a_out,
           conv_b_w, w_b_out, w_o, g_ffn, w_up, conv_f_w, w_down, g_final):
    new_a, new_b, new_f = [], [], []
    for l in range(DEPTH):
        x, na, nb, nf = _layer(x, bufs_a[l], bufs_b[l], bufs_f[l], g_mix[l], w_in[l], conv_a_w[l],
                               conv_a_b[l], ln_a_g[l], ln_a_b[l], w_a_out[l], conv_b_w[l], w_b_out[l],
                               w_o[l], g_ffn[l], w_up[l], conv_f_w[l], w_down[l])
        new_a.append(na); new_b.append(nb); new_f.append(nf)
    y = _rmsnorm(x, g_final)
    return y, jnp.stack(new_a), jnp.stack(new_b), jnp.stack(new_f)

def setup_inputs(seed: int = 0) -> dict:
    key = jax.random.key(seed)
    ks = jax.random.split(key, 24)
    f32 = jnp.float32
    nrm = lambda k, shape, s: (jax.random.normal(k, shape, f32) * s)
    return {
        "x_prompt": nrm(ks[0], (BATCH, SEQ, D_MODEL), 1.0),
        "x_sample": nrm(ks[1], (DEC_BATCH, DEC_SEQ, D_MODEL), 1.0),
        "state_conv_a": nrm(ks[2], (DEPTH, DEC_BATCH, CONV_A_W - 1, D_A), 0.5),
        "state_conv_b": nrm(ks[3], (DEPTH, DEC_BATCH, CONV_B_W - 1, D_B), 0.5),
        "state_conv_ffn": nrm(ks[4], (DEPTH, DEC_BATCH, CONV_F_W - 1, D_FF), 1.0),
        "g_mix": 1.0 + nrm(ks[5], (DEPTH, D_MODEL), 0.02),
        "w_in": nrm(ks[6], (DEPTH, D_MODEL, D_IN), D_MODEL ** -0.5),
        "conv_a_w": nrm(ks[7], (DEPTH, CONV_A_W, D_A), CONV_A_W ** -0.5),
        "conv_a_b": nrm(ks[8], (DEPTH, D_A), 0.02),
        "ln_a_g": 1.0 + nrm(ks[9], (DEPTH, D_A), 0.02),
        "ln_a_b": nrm(ks[10], (DEPTH, D_A), 0.02),
        "w_a_out": nrm(ks[11], (DEPTH, D_A, D_MODEL), D_A ** -0.5),
        "conv_b_w": nrm(ks[12], (DEPTH, CONV_B_W, D_B), CONV_B_W ** -0.5),
        "w_b_out": nrm(ks[13], (DEPTH, D_B, D_MODEL), D_B ** -0.5),
        "w_o": nrm(ks[14], (DEPTH, D_MODEL, D_MODEL), D_MODEL ** -0.5),
        "g_ffn": 1.0 + nrm(ks[15], (DEPTH, D_MODEL), 0.02),
        "w_up": nrm(ks[16], (DEPTH, D_MODEL, 2 * D_FF), D_MODEL ** -0.5),
        "conv_f_w": nrm(ks[17], (DEPTH, CONV_F_W, D_FF), CONV_F_W ** -0.5),
        "w_down": nrm(ks[18], (DEPTH, D_FF, D_MODEL), D_FF ** -0.5),
        "g_final": 1.0 + nrm(ks[19], (D_MODEL,), 0.02),
    }

def reference(x_prompt, x_sample, state_conv_a, state_conv_b, state_conv_ffn, g_mix, w_in, conv_a_w,
              conv_a_b, ln_a_g, ln_a_b, w_a_out, conv_b_w, w_b_out, w_o, g_ffn, w_up, conv_f_w,
              w_down, g_final):
    dt = x_prompt.dtype
    zeros_a = jnp.zeros((DEPTH, BATCH, CONV_A_W - 1, D_A), dt)
    zeros_b = jnp.zeros((DEPTH, BATCH, CONV_B_W - 1, D_B), dt)
    zeros_f = jnp.zeros((DEPTH, BATCH, CONV_F_W - 1, D_FF), dt)
    y_prompt, pa, pb, pf = _trunk(x_prompt, zeros_a, zeros_b, zeros_f, g_mix, w_in, conv_a_w, conv_a_b,
                                  ln_a_g, ln_a_b, w_a_out, conv_b_w, w_b_out, w_o, g_ffn, w_up,
                                  conv_f_w, w_down, g_final)
    y_sample, sa, sb, sf = _trunk(x_sample, state_conv_a, state_conv_b, state_conv_ffn, g_mix, w_in,
                                  conv_a_w, conv_a_b, ln_a_g, ln_a_b, w_a_out, conv_b_w, w_b_out, w_o,
                                  g_ffn, w_up, conv_f_w, w_down, g_final)
    return (y_prompt, y_sample, pa, pb, pf, sa, sb, sf)


_drawn_inputs = setup_inputs


def setup_inputs(seed=0):
    import zlib

    import numpy as np

    out = dict(_drawn_inputs(seed))
    spreads = {}
    factors = {'conv_a_b': 4.754, 'ln_a_g': 7.707, 'ln_a_b': 8.0, 'g_ffn': 2.911, 'g_final': 2.836}
    for name, (base, spread) in spreads.items():
        noise = np.random.default_rng([zlib.crc32(name.encode()), seed]).standard_normal(out[name].shape)
        drawn = base * np.exp(spread * noise) if base else spread * noise
        out[name] = __import__('jax').numpy.asarray(drawn.astype(out[name].dtype))
    for name, factor in factors.items():
        out[name] = (out[name] * factor).astype(out[name].dtype)
    return out
```

```python
from contextlib import ExitStack

import concourse.bass as bass
from concourse import mybir


P = 128
ALU = mybir.AluOpType
ACT = mybir.ActivationFunctionType
F32 = mybir.dt.float32
F32R = mybir.dt.float32r
X = mybir.AxisListType.X

RMS_EPS = 1e-6
LN_EPS = 1e-5
RING = 4
POOL_TAPS = 14
LATE_TAPS = 2


def build(nc, x_prompt, x_sample, state_a, state_b, state_f, g_mix, w_in, conv_a_w, conv_a_b, ln_a_g, ln_a_b,
          w_a_out, conv_b_w, w_b_out, w_o, g_ffn, w_up, conv_f_w, w_down, g_final,
          y_prompt, y_sample, a_prompt, b_prompt, f_prompt, a_sample, b_sample, f_sample):
    _, SEQ, D = x_prompt.shape
    B = x_sample.shape[0]
    WA, WB = conv_a_w.shape[1], conv_b_w.shape[1]
    FF = w_down.shape[1]
    KT = D // P
    FT = FF // P
    N = SEQ + B
    H = N // 2
    PADA, PADB = WA - 1, WB - 1
    TT = SEQ // P
    POOL_N, DVE_N = POOL_TAPS, WA - POOL_TAPS
    MIX_N = DVE_N - LATE_TAPS
    assert KT == 8 and FT == 22 and WB == 3 and N % 4 == 0 and H <= 512

    C_WA, C_BA, C_LG, C_LB, C_GM, C_GF, C_WB = 0, WA, WA + 1, WA + 2, WA + 3, WA + 4, WA + 5
    C_SB = C_WB + WB
    NC = C_SB + B * PADB
    CF_W = B * PADB
    NCF = CF_W + WB

    G_MIX, G_B, G_BOUT, G_GATE, G_AOUT, G_O, G_UP = 0, 32, 40, 48, 64, 72, 80
    G_DOWN = G_UP + 2 * FT
    KSPLIT = (6, 6, 5, 5)
    KFIRST = (0, 6, 12, 17)
    S_Q, S_V, S_M, S_H, S_G = 0, 8, 16, 24, 32

    with ExitStack() as ctx:
        def sb(name, shape, dt=F32, stack=ctx):
            return stack.enter_context(nc.sbuf_tensor(name, shape, dt))

        def sem(name):
            return ctx.enter_context(nc.semaphore(name))

        ident = sb("ident", [P, P])
        cst = sb("cst", [P, KT, NC])
        pool_prod = sb("pool_prod", [P, SEQ])
        tmp = sb("tmp", [P, 3, N])
        cx = sb("cx", [P, PADB + N])
        stat = sb("stat", [P, 24])
        raw = sb("raw", [P, RING, KT, P])
        w_hi = sb("w_hi", [P, RING, KT, P], F32R)
        w_lo = sb("w_lo", [P, RING, KT, P], F32R)
        xT = sb("xT", [P, KT, N])
        early = ExitStack()
        sb("act_tiles_0_to_7", [P, 2 * KT * N], F32R, early)
        v = sb("v", [P, KT, N], F32, early)
        gate_a = sb("gate_a", [P, KT, N], F32, early)
        y_b = sb("y_b", [P, KT, N], F32, early)
        UW = PADA + N
        u = sb("u", [P, KT, UW], F32, early)
        early.close()
        act = sb("act", [P, 2 * FT, N], F32R)
        FREE = KT * (3 * N + UW) - 2 * (FT - KT) * N
        sb("end_of_u", [P, FREE])
        middle = ExitStack()
        mid = sb("mid", [P, 2 * KT, N], F32R, middle)
        middle.close()
        y = sb("y", [P, TT + 1, D])
        gf_row = sb("gf_row", [P, D])
        sq_junk = sb("sq_junk", [P, D])
        a_pack = sb("a_pack", [P, (PADA + B) * KT])
        tail_b = sb("tail_b", [P, PADB + B, KT])
        stage = sb("stage", [P, 4, P])
        assert (TT + 3) * D + (PADA + PADB + 2 * B) * KT + 4 * P <= 2 * KT * N and (TT + 3) * D >= (2 * KT - 3) * N

        psum = ctx.enter_context(nc.psum_tensor("psum", [P, 8, 512], F32))

        uf = u[:, :, :].rearrange("p t n -> p (t n)")
        tf = tmp[:, :, :].rearrange("p t n -> p (t n)")
        vf = v[:, :, :].rearrange("p t n -> p (t n)")
        gaf = gate_a[:, :, :].rearrange("p t n -> p (t n)")
        ybf = y_b[:, :, :].rearrange("p t n -> p (t n)")
        x_tok = [vf[:, t * D:(t + 1) * D] for t in range(TT)] + [ybf[0:B, D:2 * D]]
        xn_tok = [gaf[:, t * D:(t + 1) * D] for t in range(TT)] + [ybf[0:B, 2 * D:3 * D]]
        crow = ybf[0:NC, 0:D]
        u0 = KT * UW - FREE
        frow = uf[0:NCF, 0:FF]
        rinv = uf[:, u0:u0 + N]
        up_n = uf[:, u0 + N:u0 + 2 * N]
        cst_f = uf[:, u0 + 2 * N:u0 + 2 * N + FT * NCF].rearrange("p (t c) -> p t c", c=NCF)
        s2_at = u0 + 2 * N + FT * NCF
        ssum = uf[:, s2_at:s2_at + N]
        ones = uf[:, s2_at + N:s2_at + N + P]
        assert s2_at + N + P <= KT * UW and FF <= u0 + 2 * N
        tail_f = cst[:, :, :].rearrange("p t c -> p (t c)")[:, 0:(PADB + B) * FT].rearrange("p (r t) -> p r t", t=FT)
        t0, t1, t2 = (tmp[:, k, :] for k in range(3))
        win = t0[:, 0:B * WA].rearrange("p (b k) -> p b k", k=WA)
        win_w = t1[:, 0:B * WA].rearrange("p (b k) -> p b k", k=WA)
        SH = B * PADA // 2
        assert SH == PADA * KT // 2
        st_row = t1[0:SH, B * WA:B * WA + 2 * P].rearrange("p (h c) -> p h c", h=2)
        f_stage = [t2[:, j * P:(j + 1) * P] for j in range(3)]
        vsum = cx[:, 0:N]
        ms, rs = stat[:, 0:5], stat[:, 5:10]
        win_sum = stat[:, 10:18]

        x_in = [sem(f"x_in{t}") for t in range(TT + 1)]
        rows_in, frows_in, state_in, gf_in = sem("rows_in"), sem("frows_in"), sem("state_in"), sem("gf_in")
        raw_in = [sem(f"raw_in{s}") for s in range(RING)]
        const_set, ident_set = sem("const_set"), sem("ident_set")
        cst_turned, cst_done = sem("cst_turned"), sem("cst_done")
        x_squared, x_mean, x_root, x_inv, xn_done = (sem(n) for n in ("x_squared", "x_mean", "x_root", "x_inv", "xn_done"))
        x_turned, xT_done, hg_done, h_hi, h_lo = (sem(n) for n in ("x_turned", "xT_done", "hg_done", "h_hi", "h_lo"))
        hi_done, lo_done, mm_done, evicted = sem("hi_done"), sem("lo_done"), sem("mm_done"), sem("evicted")
        act_hi, act_lo, prod_done = sem("act_hi"), sem("act_lo"), sem("prod_done")
        u_done, pool_mul, pool_sum, dve_tap, conv_b, tail_b_done = (sem(n) for n in ("u_done", "pool_mul", "pool_sum", "dve_tap", "conv_b", "tail_b_done"))
        a_packed, a_turned, a_staged, state_turned, win_done, win_conv, v_done = (
            sem(n) for n in ("a_packed", "a_turned", "a_staged", "state_turned", "win_done", "win_conv", "v_done"))
        sum_zero, vsum_done, mean_done, frow_turned, cst_f_done = (
            sem(n) for n in ("sum_zero", "vsum_done", "mean_done", "frow_turned", "cst_f_done"))
        centred, squared, ssum_done, var_done, var_eps, var_root, rinv_done = (
            sem(n) for n in ("centred", "squared", "ssum_done", "var_done", "var_eps", "var_root", "rinv_done"))
        yb_gated, v_norm, v_sig, v_affine, table_set = (sem(n) for n in ("yb_gated", "v_norm", "v_sig", "v_affine", "table_set"))
        conv_f, fg_tail, silu_done = sem("conv_f"), sem("fg_tail"), sem("silu_done")
        f_turned, f_staged = sem("f_turned"), sem("f_staged")
        y_turned, y_copied, y_squared, y_stat, y_root, y_inv, y_done = (
            sem(n) for n in ("y_turned", "y_copied", "y_squared", "y_stat", "y_root", "y_inv", "y_done"))
        state_out = sem("state_out")
        y_out = sem("y_out")

        def out_of(t):
            return t + 2

        def halves(ap):
            return ap.rearrange("p (a b) -> p a b", a=2)

        def tile(t, i, lo=0, hi=None):
            hi = t.shape[2] if hi is None else hi
            return t[:, bass.ds(i, 1), lo:hi].rearrange("p o n -> p (o n)")

        def scal(t, i, c):
            return t[:, bass.ds(i, 1), c:c + 1].rearrange("p o c -> p (o c)")

        def acc(s):
            return psum[:, 2 * (s % 2):2 * (s % 2) + 2, 0:H]

        stat_banks = psum[:, 6:8, 0:H]

        def kview(w, rows=None):
            w = w[0] if rows is None else w[0, rows[0]:rows[1], :]
            return w.rearrange("(k p) n -> p k n", p=P)

        wi = kview(w_in)
        COL = {"a_val": 0, "a_gate": D, "b_B": 2 * D, "b_C": 3 * D, "b_x": 4 * D, "g_A": 5 * D, "g_B": 6 * D}

        block = ctx.enter_context(nc.Block())

        @block.sync
        def _(sp):
            for t in range(TT):
                sp.dma_start(x_tok[t], x_prompt[0, t * P:(t + 1) * P, :]).then_inc(x_in[t], 16)
            sp.dma_start(x_tok[TT], x_sample.rearrange("b s d -> (b s) d")).then_inc(x_in[TT], 16)

            def load(g, s, src, k=KT):
                sp.wait_ge(lo_done, g - (RING - 1))
                sp.dma_start(raw[:, s, 0:k, :], src).then_inc(raw_in[s], 16)

            def pairs(first, names, w, it):
                for s in range(4):
                    c = names[s % 2] + (s // 2) * P + 2 * P * it
                    load(first + s, s, w[:, :, bass.ds(c, P)])

            for s in range(RING):
                c = (COL["a_val"], COL["a_gate"])[s % 2] + (s // 2) * P
                sp.dma_start(raw[:, s, :, :], wi[:, :, c:c + P]).then_inc(raw_in[s], 16)
            pairs(G_MIX + 4, (COL["b_C"], COL["b_x"]), wi, 0)
            with sp.Fori(1, KT // 2) as it:
                pairs(G_MIX + 8 * it, (COL["a_val"], COL["a_gate"]), wi, it)
                pairs(G_MIX + 8 * it + 4, (COL["b_C"], COL["b_x"]), wi, it)

            def plain(first, w, col):
                with sp.Fori(0, KT // RING) as it:
                    for s in range(RING):
                        load(first + RING * it + s, s, w[:, :, bass.ds(col + s * P + RING * P * it, P)])

            plain(G_B, wi, COL["b_B"])
            plain(G_BOUT, kview(w_b_out), 0)
            with sp.Fori(0, KT // 2) as it:
                pairs(G_GATE + 4 * it, (COL["g_A"], COL["g_B"]), wi, it)
            plain(G_AOUT, kview(w_a_out), 0)
            plain(G_O, kview(w_o), 0)
            wu = kview(w_up)
            with sp.Fori(0, FT // 2) as it:
                pairs(G_UP + 4 * it, (0, FF), wu, it)
            wd = kview(w_down)
            with sp.Fori(0, KT) as n:
                for s in range(RING):
                    load(G_DOWN + RING * n + s, s,
                         wd[:, KFIRST[s]:KFIRST[s] + KSPLIT[s], bass.ds(P * n, P)], KSPLIT[s])

            sp.wait_ge(mm_done, G_DOWN)
            sp.dma_start(gf_row[:, :], g_final.rearrange("(o d) -> o d", o=1).broadcast_to([P, D])).then_inc(gf_in, 16)
            for t in range(TT + 1):
                sp.wait_ge(y_done, t + 1)
                if t < TT:
                    sp.dma_start(y_prompt[0, t * P:(t + 1) * P, :], y[:, t, :]).then_inc(y_out, 16)
                else:
                    sp.dma_start(y_sample.rearrange("b s d -> (b s) d"), y[0:B, TT, :]).then_inc(y_out, 16)
            sp.wait_ge(y_out, 16 * (TT + 1))
            sp.wait_ge(state_out, 16 * 11)

        @block.gpsimd
        def _(pool):
            pool.memset(ident[:, :], 0.0).then_inc(ident_set, 1)
            pool.wait_ge(ident_set, 1)
            pool.affine_select(out=ident[:, :], in_=ident[:, :], compare_op=ALU.not_equal, fill=1.0, base=0,
                               pattern=[[-1, P]], channel_multiplier=1).then_inc(ident_set, 1)
            pool.memset(u[:, :, 0:PADA], 0.0).then_inc(const_set, 1)
            pool.memset(cx[:, 0:PADB], 0.0).then_inc(const_set, 1)
            pool.wait_ge(const_set, 3)
            for i in range(KT):
                pool.wait_ge(u_done, i + 1)
                part = gate_a[:, i, 0:SEQ]
                for k in range(POOL_N):
                    src, w = u[:, i, k:k + SEQ], cst[:, i, C_WA + k:C_WA + k + 1]
                    if k == 0:
                        pool.tensor_scalar(part, src, w, None, ALU.mult).then_inc(pool_sum, 1)
                        continue
                    pool.wait_ge(pool_sum, POOL_N * i + k)
                    pool.tensor_scalar(pool_prod[:, :], src, w, None, ALU.mult).then_inc(pool_mul, 1)
                    pool.wait_ge(pool_mul, (POOL_N - 1) * i + k)
                    pool.tensor_tensor(part, part, pool_prod[:, :], ALU.add).then_inc(pool_sum, 1)

        @block.scalar
        def _(sc):
            for r, n, src in ((C_WA, WA, conv_a_w[0]), (C_BA, 1, conv_a_b), (C_LG, 1, ln_a_g), (C_LB, 1, ln_a_b),
                              (C_GM, 1, g_mix), (C_GF, 1, g_ffn), (C_WB, WB, conv_b_w[0]),
                              (C_SB, B * PADB, state_b[0].rearrange("b k c -> (b k) c"))):
                sc.dma_start(crow[r:r + n, :], src).then_inc(rows_in, 16)
            for old, new in ((state_a, a_sample), (state_b, b_sample), (state_f, f_sample)):
                k = old.shape[2]
                sc.dma_start(new[0, :, 0:k - 1, :], old[0, :, 1:k, :]).then_inc(state_out, 16)

            def hi_split(g, s, k=KT, first=False):
                if first:
                    sc.wait_ge(raw_in[s], 16)
                else:
                    sc.wait_ge(raw_in[s], (g - s) * (16 // RING) + 16)
                    sc.wait_ge(mm_done, g - (RING - 1))
                sc.activation(w_hi[:, s, 0:k, :], raw[:, s, 0:k, :], ACT.Copy).then_inc(hi_done, 1)

            def evict(g, t, out, func):
                sc.wait_ge(mm_done, g + 1)
                sc.wait_ge(evicted, out_of(t - 1))
                sc.activation(halves(out), acc(g_slot[0]), func).then_inc(evicted, 1)

            g_slot = [0]

            def h_part(t):
                n = P if t < TT else B
                base = 4 if t % 2 == 0 else 0
                cols = slice(t * P, t * P + n)
                for b in range(2):
                    if b == 0:
                        sc.wait_ge(x_turned, 2 * t + 1)
                    sc.activation(xT[:, 4 * b:4 * b + 4, cols],
                                  psum[:, base + b, :].rearrange("p (k n) -> p k n", k=4)[:, :, 0:n],
                                  ACT.Copy).then_inc(xT_done, 1)
                for b in range(2):
                    sc.wait_ge(hg_done, 2 * t + b + 1)
                    hg = (t2 if b == 0 else cx[:, PADB:PADB + N])[:, 0:4 * n].rearrange("p (k n) -> p k n", k=4)
                    sc.activation(act[:, 8 * b:8 * b + 8:2, cols], hg, ACT.Copy).then_inc(h_hi, 1)

            sc.wait_ge(const_set, 3)
            for t in range(TT + 1):
                n = P if t < TT else B
                sc.wait_ge(x_in[t], 16)
                if t > 0:
                    sc.wait_ge(x_squared, t)
                sc.activation(tf[0:n, 0:D], x_tok[t], ACT.Square, accum_out=stat[0:n, 18 + t:19 + t]).then_inc(x_squared, 1)
                if t == 0:
                    sc.wait_ge(cst_turned, 1)
                    sc.activation(cst[:, :, :], psum[:, 3, 0:KT * NC].rearrange("p (t c) -> p t c", c=NC),
                                  ACT.Copy).then_inc(cst_done, 1)
                sc.wait_ge(x_mean, t + 1)
                sc.activation(rs[0:n, t:t + 1], ms[0:n, t:t + 1], ACT.Sqrt).then_inc(x_root, 1)
                if t > 0:
                    h_part(t - 1)
            h_part(TT)
            for s in range(RING):
                hi_split(s, s, first=True)
            sc.activation(rs, ms, ACT.Sigmoid).then_inc(table_set, 1)

            with sc.Fori(0, KT // 2) as it:
                for s in range(8):
                    g = G_MIX + 8 * it + s
                    g_slot[0] = s
                    i = 2 * it + (s % 4) // 2
                    if s in (0, 2, 1, 3):
                        sc.wait_ge(u_done, i)
                        evict(g, g, t0 if s % 2 == 0 else t1, ACT.Copy if s % 2 == 0 else ACT.Sigmoid)
                    elif s % 2 == 0:
                        sc.wait_ge(u_done, 2 * it + 2)
                        evict(g, g, t0, ACT.Copy)
                    hi_split(g + RING, s % RING)
                    if s in (5, 7):
                        sc.wait_ge(evicted, out_of(g))
                        sc.activation(tail_b[:, :, bass.ds(i, 1)].rearrange("p r o -> p (r o)"), cx[:, SEQ:SEQ + PADB + B],
                                      ACT.Copy).then_inc(tail_b_done, 1)

            a_rows = a_prompt[0, 0].rearrange("r (t c) -> (r t) c", c=P)
            sc.wait_ge(u_done, KT)
            sc.dma_start(st_row, state_a[0].rearrange("b k c -> (b k) c")[:, 0:P].rearrange("(h p) c -> p h c", h=2)).then_inc(state_in, 16)
            for c, n, first in ((0, PADA, SEQ), (PADA * KT, B, PADA + SEQ)):
                sc.activation(a_pack[:, c:c + n * KT].rearrange("p (r t) -> p t r", t=KT), u[:, :, first:first + n],
                              ACT.Copy).then_inc(a_packed, 1)
            na, nb = SH, PADB * KT
            for j, n in enumerate((na, na, B * KT, nb + B * KT)):
                sc.wait_ge(a_turned, j + 1)
                sc.activation(stage[0:n, j, :], psum[0:n, (5, 6, 7, 4)[j], 0:P], ACT.Copy).then_inc(a_staged, 1)
            rows = lambda ap: ap.rearrange("r (t c) -> (r t) c", c=P)
            last_rows = lambda ap, k: ap[0, :, k - 1, :].rearrange("b (t c) -> b t c", c=P)
            for j, out, src in ((0, a_rows[0:na, :], stage[0:na, 0, :]), (1, a_rows[na:2 * na, :], stage[0:na, 1, :]),
                                (2, last_rows(a_sample, PADA), stage[0:B * KT, 2, :]),
                                (3, rows(b_prompt[0, 0]), stage[0:nb, 3, :]),
                                (3, last_rows(b_sample, PADB), stage[nb:nb + B * KT, 3, :])):
                sc.wait_ge(a_staged, j + 1)
                sc.dma_start(out, src).then_inc(state_out, 16)

            def state_tile(i, last=False):
                sc.wait_ge(state_turned, i + 1)
                sc.wait_ge(win_conv, 3 * i)
                sc.activation(win[:, :, 0:PADA], psum[:, 4, 0:B * PADA].rearrange("p (b k) -> p b k", k=PADA),
                              ACT.Copy).then_inc(win_done, 1)
                sc.activation(win[:, :, PADA:WA].rearrange("p b k -> p (b k)"), tile(u, i, PADA + SEQ, UW),
                              ACT.Copy).then_inc(win_done, 1)
                if not last:
                    src = state_a[0].rearrange("b k c -> (b k) c")[:, bass.ds(P * i + P, P)]
                    sc.dma_start(st_row, src.rearrange("(h p) c -> p h c", h=2)).then_inc(state_in, 16)

            def act_hi_split(out, src, sem_, value, scale=None):
                sc.wait_ge(sem_, value)
                if scale is None:
                    sc.activation(out, src, ACT.Copy).then_inc(act_hi, 1)
                else:
                    sc.activation(out, src, ACT.Copy, scale=scale).then_inc(act_hi, 1)

            def b_step(i, s, last=False):
                hi_split(G_B + RING + i, s)
                state_tile(i, last)
                act_hi_split(tile(mid, 2 * i), t2, evicted, out_of(G_B + i))

            with sc.Fori(0, KT // RING - 1) as it:
                for s in range(RING):
                    b_step(RING * it + s, s)
            for s in range(RING):
                if s == 2:
                    sc.wait_ge(state_out, 16 * 8)
                b_step(KT - RING + s, s, last=s == RING - 1)

            with sc.Fori(0, KT // RING) as it:
                for s in range(RING):
                    g_slot[0] = s
                    i = RING * it + s
                    evict(G_BOUT + i, G_BOUT + i, tile(y_b, i), ACT.Copy)
                    hi_split(G_BOUT + RING + i, s)
            sc.wait_ge(v_done, KT)
            sc.wait_ge(win_done, 2 * KT)
            sc.dma_start(frow[0:CF_W, :], state_f[0].rearrange("b k c -> (b k) c")).then_inc(frows_in, 16)
            sc.dma_start(frow[CF_W:NCF, :], conv_f_w[0]).then_inc(frows_in, 16)
            sc.wait_ge(frow_turned, 1)
            sc.activation(cst_f, psum[:, 4, 0:FT * NCF].rearrange("p (t c) -> p t c", c=NCF), ACT.Copy).then_inc(cst_f_done, 1)

            def gate_step(it, s):
                g = G_GATE + RING * it + s
                g_slot[0] = s
                i = 2 * it + s // 2
                if s % 2 == 0:
                    evict(g, g, tile(gate_a, i), ACT.Sigmoid)
                else:
                    sc.wait_ge(yb_gated, i)
                    evict(g, g, t1, ACT.Sigmoid)
                hi_split(g + RING, s)

            with sc.Fori(0, 2) as it:
                for s in range(RING):
                    gate_step(it, s)
                    t = RING * it + s
                    sc.wait_ge(centred, t + 1)
                    sc.wait_ge(ssum_done, t)
                    sc.activation(t0, tile(v, t), ACT.Square).then_inc(squared, 1)
            sc.wait_ge(var_eps, 1)
            sc.activation(rinv, rinv, ACT.Sqrt).then_inc(var_root, 1)
            sc.activation(rs, ms, ACT.Sigmoid).then_inc(table_set, 1)
            with sc.Fori(2, 4) as it:
                for s in range(RING):
                    gate_step(it, s)
                    t = RING * it - 2 * RING + s
                    sc.wait_ge(v_norm, t + 1)
                    sc.wait_ge(prod_done, t)
                    sc.activation(t0, tile(v, t), ACT.Sigmoid, scale=scal(cst, t, C_LG),
                                  bias=scal(cst, t, C_LB)).then_inc(v_sig, 1)
                    act_hi_split(tile(mid, 2 * t), t2, prod_done, t + 1)

            with sc.Fori(0, KT // RING) as it:
                for s in range(RING):
                    i = RING * it + s
                    hi_split(G_AOUT + RING + i, s)
                    act_hi_split(tile(act, 2 * i), t2, prod_done, KT + i + 1)

            with sc.Fori(0, KT // RING) as it:
                for s in range(RING):
                    i = RING * it + s
                    hi_split(G_O + RING + i, s)
                    sc.wait_ge(ssum_done, KT + i)
                    act_hi_split(tile(mid, 2 * i), tile(xT, i), evicted, out_of(G_O + i), scal(cst, i, C_GF))
                    sc.activation(t0, tile(xT, i), ACT.Square).then_inc(squared, 1)
            sc.wait_ge(var_eps, 2)
            sc.activation(rinv, rinv, ACT.Sqrt).then_inc(var_root, 1)
            sc.activation(rs, ms, ACT.Silu).then_inc(table_set, 1)

            with sc.Fori(0, FT // 2) as it:
                for s in range(RING):
                    g = G_UP + RING * it + s
                    i = 2 * it + s // 2
                    hi_split(g + RING, s)
                    if s % 2 == 0:
                        sc.wait_ge(evicted, out_of(g))
                        sc.activation(tail_f[:, :, bass.ds(i, 1)].rearrange("p r o -> p (r o)"),
                                      cx[:, SEQ:SEQ + PADB + B], ACT.Copy).then_inc(fg_tail, 1)
                        sc.wait_ge(conv_f, 6 * i + 6)
                        sc.wait_ge(prod_done, 2 * KT + i)
                        sc.activation(t1, t0, ACT.Silu).then_inc(silu_done, 1)
                    else:
                        act_hi_split(tile(act, 2 * i), t2, prod_done, 2 * KT + i + 1)

            nf, hb = PADB * FT, B // 2
            sc.wait_ge(act_lo, S_G + FT)
            for j in range(3):
                sc.wait_ge(f_turned, j + 1)
                n = nf if j == 0 else hb * FT
                sc.activation(f_stage[j][0:n, :], psum[0:n, 4 + j, 0:P], ACT.Copy).then_inc(f_staged, 1)
                sc.wait_ge(f_staged, j + 1)
                if j == 0:
                    sc.dma_start(f_prompt[0, 0].rearrange("r (t c) -> (r t) c", c=P), f_stage[j][0:n, :]).then_inc(state_out, 16)
                else:
                    sc.dma_start(f_sample[0, (j - 1) * hb:j * hb, PADB - 1, :].rearrange("b (t c) -> b t c", c=P),
                                 f_stage[j][0:n, :]).then_inc(state_out, 16)
            sc.activation(rs, ms, ACT.Sqrt).then_inc(table_set, 1)

            def y_tile(n, par):
                sc.wait_ge(y_turned, n + 1)
                main = psum[:, 4 + 2 * par, :].rearrange("p (t c) -> p t c", c=P)
                side = psum[0:B, 5 + 2 * par, 0:P]
                sc.activation(y[:, 0:TT, bass.ds(P * n, P)], main, ACT.Copy).then_inc(y_copied, 1)
                sc.activation(y[0:B, TT, bass.ds(P * n, P)], side, ACT.Copy).then_inc(y_copied, 1)

            def down_split(n, s):
                hi_split(G_DOWN + RING * n + RING + s, s, KSPLIT[s])

            with sc.Fori(0, KT // 2 - 1) as it:
                for par in range(2):
                    for s in range(RING):
                        down_split(2 * it + par, s)
                    y_tile(2 * it + par, par)
            for s in range(RING):
                down_split(KT - 2, s)
            y_tile(KT - 2, 0)
            y_tile(KT - 1, 1)
            for t in range(TT + 1):
                n = P if t < TT else B
                sc.wait_ge(y_copied, 2 * KT)
                if t > 0:
                    sc.wait_ge(y_squared, t)
                sc.activation(sq_junk[0:n, :], y[0:n, t, :], ACT.Square, accum_out=stat[0:n, 18 + t:19 + t]).then_inc(y_squared, 1)
                sc.wait_ge(y_stat, t + 1)
                sc.activation(rs[0:n, t:t + 1], ms[0:n, t:t + 1], ACT.Sqrt).then_inc(y_root, 1)

        @block.vector
        def _(ve):
            ve.memset(stat[:, :], 1.0).then_inc(const_set, 1)

            def lo_split(g, s, k=KT, first=False):
                ve.wait_ge(hi_done, g + 1)
                if not first:
                    ve.wait_ge(mm_done, g - (RING - 1))
                ve.tensor_tensor(w_lo[:, s, 0:k, :], raw[:, s, 0:k, :], w_hi[:, s, 0:k, :], ALU.subtract).then_inc(lo_done, 1)

            def act_lo_split(out, src, hi, a):
                ve.wait_ge(act_hi, a + 1)
                ve.tensor_tensor(out, src, hi, ALU.subtract).then_inc(act_lo, 1)

            def out_of_psum(g, t):
                ve.wait_ge(mm_done, g + 1)
                ve.wait_ge(evicted, out_of(t - 1))

            def h_part(t):
                n = P if t < TT else B
                base = 6 if t % 2 == 0 else 2
                cols = slice(t * P, t * P + n)
                ve.wait_ge(x_turned, 2 * t + 2)
                for b in range(2):
                    if t > 0:
                        ve.wait_ge(h_lo, 2 * t - 1 + b)
                    hg = (t2 if b == 0 else cx[:, PADB:PADB + N])[:, 0:4 * n].rearrange("p (k n) -> p k n", k=4)
                    g = cst[:, 4 * b:4 * b + 4, C_GM:C_GM + 1].broadcast_to([P, 4, n])
                    ve.tensor_tensor(hg, psum[:, base + b, :].rearrange("p (k n) -> p k n", k=4)[:, :, 0:n], g,
                                     ALU.mult).then_inc(hg_done, 1)
                for b in range(2):
                    ve.wait_ge(h_hi, 2 * t + b + 1)
                    hg = (t2 if b == 0 else cx[:, PADB:PADB + N])[:, 0:4 * n].rearrange("p (k n) -> p k n", k=4)
                    ve.tensor_tensor(act[:, 8 * b + 1:8 * b + 8:2, cols], hg, act[:, 8 * b:8 * b + 8:2, cols],
                                     ALU.subtract).then_inc(h_lo, 1)

            for t in range(TT + 1):
                n = P if t < TT else B
                ve.wait_ge(x_squared, t + 1)
                ve.tensor_scalar(ms[0:n, t:t + 1], stat[0:n, 18 + t:19 + t], 1.0 / D, RMS_EPS, ALU.mult, ALU.add).then_inc(x_mean, 1)
                ve.wait_ge(x_root, t + 1)
                ve.reciprocal(rs[0:n, t:t + 1], rs[0:n, t:t + 1]).then_inc(x_inv, 1)
                ve.wait_ge(x_inv, t + 1)
                ve.tensor_scalar(xn_tok[t], x_tok[t], rs[0:n, t:t + 1], None, ALU.mult).then_inc(xn_done, 1)
                if t == 0:
                    ve.wait_ge(cst_done, 1)
                    ve.wait_ge(const_set, 3)
                else:
                    h_part(t - 1)
            h_part(TT)
            ve.memset(stat[:, 23:24], 0.0).then_inc(evicted, 1)
            for s in range(RING):
                lo_split(s, s, first=True)

            def taps(i, first, last):
                for k in range(first, last):
                    src, w = tile(u, i, POOL_N + k, POOL_N + k + SEQ), scal(cst, i, C_WA + POOL_N + k)
                    out = tile(v, i, 0, SEQ)
                    if k == 0:
                        ve.wait_ge(u_done, i + 1)
                        ve.tensor_scalar(out, src, w, scal(cst, i, C_BA), ALU.mult, ALU.add).then_inc(dve_tap, 1)
                        continue
                    if k < MIX_N:
                        ve.wait_ge(dve_tap, MIX_N * i + k)
                    elif k > MIX_N:
                        ve.wait_ge(dve_tap, MIX_N * KT + LATE_TAPS * i + k - MIX_N)
                    ve.scalar_tensor_tensor(out=out, in0=src, scalar=w, in1=out, op0=ALU.mult,
                                            op1=ALU.add).then_inc(dve_tap, 1)

            def narrow(i, out_main, out_side, w, w_c, state, s_c, done):
                for k in range(WB):
                    wk = scal(w, i, w_c + k)
                    side = cx[:, PADB + SEQ:PADB + N] if k == PADB else \
                        state[:, bass.ds(i, 1), s_c + k:s_c + B * PADB:PADB].rearrange("p o b -> p (o b)")
                    for j, (out, src) in enumerate(((out_main, cx[:, k:k + SEQ]), (out_side, side))):
                        if k == 0:
                            ve.tensor_scalar(out, src, wk, None, ALU.mult).then_inc(done, 1)
                        else:
                            ve.wait_ge(done, 6 * i + 2 * k + j - 1)
                            ve.scalar_tensor_tensor(out=out, in0=src, scalar=wk, in1=out, op0=ALU.mult,
                                                    op1=ALU.add).then_inc(done, 1)

            cuts = {1: ((0, 0, 5),), 2: ((0, 5, 11),), 3: ((0, 11, MIX_N), (1, 0, 1)), 4: ((1, 1, 7),), 5: ((1, 7, 8),),
                    6: ((1, 8, MIX_N - 1),), 7: ((1, MIX_N - 1, MIX_N),)}
            with ve.Fori(0, KT // 2) as it:
                for s in range(8):
                    g = G_MIX + 8 * it + s
                    i = 2 * it + (s % 4) // 2
                    if s in (1, 3):
                        ve.wait_ge(evicted, out_of(g))
                        ve.tensor_tensor(tile(u, i, PADA, UW), t0, t1, ALU.mult).then_inc(u_done, 1)
                    if s in (5, 7):
                        out_of_psum(g, g)
                        ve.wait_ge(tail_b_done, i)
                        ve.wait_ge(conv_b, 6 * i)
                        ve.tensor_tensor(halves(cx[:, PADB:PADB + N]), acc(s), halves(t0), ALU.mult).then_inc(evicted, 1)
                    lo_split(g + RING, s % RING)
                    if s in (5, 7):
                        ve.wait_ge(evicted, out_of(g))
                        narrow(i, tile(y_b, i, 0, SEQ), tile(y_b, i, SEQ, N), cst, C_WB, cst, C_SB, conv_b)
                    for odd, a, b in cuts.get(s, ()):
                        taps(2 * it + odd, a, b)

            with ve.Fori(0, KT // RING) as it:
                for s in range(RING):
                    i = RING * it + s
                    out_of_psum(G_B + i, G_B + i)
                    ve.wait_ge(act_lo, i)
                    ve.wait_ge(conv_b, 6 * KT)
                    ve.tensor_tensor(halves(t2), acc(s), halves(tile(y_b, i)), ALU.mult).then_inc(evicted, 1)
                    lo_split(G_B + RING + i, s)
                    ve.wait_ge(win_done, 2 * i + 2)
                    wa = cst[:, bass.ds(i, 1), C_WA:C_WA + WA].broadcast_to([P, B, WA])
                    ve.tensor_tensor(win_w, win, wa, ALU.mult).then_inc(win_conv, 1)
                    ve.wait_ge(win_conv, 3 * i + 1)
                    ve.tensor_reduce(win_sum, win_w, X, ALU.add).then_inc(win_conv, 1)
                    act_lo_split(tile(mid, 2 * i + 1), t2, tile(mid, 2 * i), S_Q + i)
                    ve.wait_ge(win_conv, 3 * i + 2)
                    ve.tensor_scalar(tile(v, i, SEQ, N), win_sum, scal(cst, i, C_BA), None, ALU.add).then_inc(win_conv, 1)

            ve.wait_ge(tail_b_done, KT)
            ve.memset(vsum, 0.0).then_inc(sum_zero, 1)
            ve.wait_ge(sum_zero, 1)
            ve.wait_ge(dve_tap, MIX_N * KT)
            ve.wait_ge(win_conv, 3 * KT)
            with ve.Fori(0, KT // RING) as it:
                for s in range(RING):
                    i = RING * it + s
                    taps(i, MIX_N, DVE_N)
                    lo_split(G_BOUT + RING + i, s)
                    ve.wait_ge(pool_sum, POOL_N * i + POOL_N)
                    ve.wait_ge(dve_tap, MIX_N * KT + LATE_TAPS * i + LATE_TAPS)
                    ve.tensor_tensor(tile(v, i, 0, SEQ), tile(v, i, 0, SEQ), tile(gate_a, i, 0, SEQ), ALU.add).then_inc(v_done, 1)
                    ve.wait_ge(v_done, i + 1)
                    ve.wait_ge(vsum_done, i)
                    ve.tensor_tensor(vsum, vsum, tile(v, i), ALU.add).then_inc(vsum_done, 1)
            ve.memset(ones, 1.0 / D).then_inc(sum_zero, 1)
            ve.memset(ssum, 0.0).then_inc(sum_zero, 1)
            ve.wait_ge(sum_zero, 3)

            def gate_step(it, s):
                g = G_GATE + RING * it + s
                if s % 2 == 1:
                    i = 2 * it + s // 2
                    ve.wait_ge(evicted, out_of(g))
                    ve.tensor_tensor(tile(y_b, i), tile(y_b, i), t1, ALU.mult).then_inc(yb_gated, 1)
                lo_split(g + RING, s)

            def square_sum(t, at):
                ve.wait_ge(squared, at + t + 1)
                ve.wait_ge(ssum_done, at + t)
                ve.tensor_tensor(ssum, ssum, t0, ALU.add).then_inc(ssum_done, 1)

            def root(n, eps):
                ve.wait_ge(var_done, n)
                ve.tensor_scalar(halves(rinv), stat_banks, eps, None, ALU.add).then_inc(var_eps, 1)
                ve.wait_ge(var_root, n)
                ve.reciprocal(rinv, rinv).then_inc(rinv_done, 1)
                ve.wait_ge(rinv_done, n)

            ve.wait_ge(mean_done, 1)
            with ve.Fori(0, 2) as it:
                for s in range(RING):
                    t = RING * it + s
                    ve.tensor_tensor(halves(tile(v, t)), halves(tile(v, t)), stat_banks, ALU.subtract).then_inc(centred, 1)
                    gate_step(it, s)
                    square_sum(t, 0)
            ve.wait_ge(frow_turned, 1)
            root(1, LN_EPS)
            ve.memset(ssum, 0.0).then_inc(sum_zero, 1)
            with ve.Fori(2, 4) as it:
                for s in range(RING):
                    t = RING * it - 2 * RING + s
                    ve.wait_ge(centred, KT)
                    ve.tensor_tensor(tile(v, t), tile(v, t), rinv, ALU.mult).then_inc(v_norm, 1)
                    gate_step(it, s)
                    ve.wait_ge(v_sig, t + 1)
                    ve.tensor_scalar(tile(v, t), tile(v, t), scal(cst, t, C_LG), scal(cst, t, C_LB), ALU.mult,
                                     ALU.add).then_inc(v_affine, 1)
                    ve.wait_ge(v_affine, t + 1)
                    ve.wait_ge(act_lo, S_V + t)
                    ve.tensor_tensor(t2, tile(v, t), t0, ALU.mult).then_inc(prod_done, 1)
                    act_lo_split(tile(mid, 2 * t + 1), t2, tile(mid, 2 * t), S_V + t)

            ve.wait_ge(yb_gated, KT)
            with ve.Fori(0, KT // RING) as it:
                for s in range(RING):
                    i = RING * it + s
                    g = G_AOUT + i
                    out_of_psum(g, g)
                    ve.wait_ge(prod_done, KT + i)
                    ve.tensor_tensor(halves(t1), acc(s), halves(tile(gate_a, i)), ALU.mult).then_inc(evicted, 1)
                    ve.wait_ge(evicted, out_of(g))
                    ve.wait_ge(act_lo, S_M + i)
                    ve.tensor_tensor(t2, t1, tile(y_b, i), ALU.add).then_inc(prod_done, 1)
                    lo_split(g + RING, s)
                    act_lo_split(tile(act, 2 * i + 1), t2, tile(act, 2 * i), S_M + i)

            ve.wait_ge(sum_zero, 4)
            with ve.Fori(0, KT // RING) as it:
                for s in range(RING):
                    i = RING * it + s
                    g = G_O + i
                    out_of_psum(g, g)
                    ve.tensor_tensor(halves(tile(xT, i)), acc(s), halves(tile(xT, i)), ALU.add).then_inc(evicted, 1)
                    lo_split(g + RING, s)
                    ve.wait_ge(act_hi, S_H + i + 1)
                    ve.wait_ge(evicted, out_of(g))
                    ve.scalar_tensor_tensor(out=tile(mid, 2 * i + 1), in0=tile(xT, i), scalar=scal(cst, i, C_GF),
                                            in1=tile(mid, 2 * i), op0=ALU.mult, op1=ALU.subtract).then_inc(act_lo, 1)
                    square_sum(i, KT)
            root(2, RMS_EPS)
            ve.memset(cx[:, 0:PADB], 0.0).then_inc(sum_zero, 1)
            ve.wait_ge(sum_zero, 5)
            ve.wait_ge(cst_f_done, 1)

            with ve.Fori(0, FT // 2) as it:
                for s in range(RING):
                    g = G_UP + RING * it + s
                    i = 2 * it + s // 2
                    out_of_psum(g, g)
                    if s % 2 == 0:
                        ve.wait_ge(fg_tail, i)
                        ve.wait_ge(conv_f, 6 * i)
                        ve.wait_ge(silu_done, i)
                        ve.tensor_tensor(halves(cx[:, PADB:PADB + N]), acc(s), halves(rinv), ALU.mult).then_inc(evicted, 1)
                        ve.wait_ge(evicted, out_of(g))
                        narrow(i, t0[:, 0:SEQ], t0[:, SEQ:N], cst_f, CF_W, cst_f, 0, conv_f)
                        lo_split(g + RING, s)
                    else:
                        ve.tensor_tensor(halves(up_n), acc(s), halves(rinv), ALU.mult).then_inc(evicted, 1)
                        ve.wait_ge(evicted, out_of(g))
                        ve.wait_ge(silu_done, i + 1)
                        ve.wait_ge(act_lo, S_G + i)
                        ve.tensor_tensor(t2, up_n, t1, ALU.mult).then_inc(prod_done, 1)
                        lo_split(g + RING, s)
                        act_lo_split(tile(act, 2 * i + 1), t2, tile(act, 2 * i), S_G + i)

            def down(n, par, split):
                if split:
                    for s in range(RING):
                        lo_split(G_DOWN + RING * n + RING + s, s, KSPLIT[s])
                ve.wait_ge(mm_done, G_DOWN + RING * n + RING)
                ve.wait_ge(evicted, out_of(G_DOWN + n - 1))
                ve.wait_ge(y_turned, n)
                out = (t0, t1)[par]
                ve.tensor_tensor(halves(out), acc(par), halves(tile(xT, n)), ALU.add).then_inc(evicted, 1)

            with ve.Fori(0, KT // 2 - 1) as it:
                for par in range(2):
                    down(2 * it + par, par, True)
            down(KT - 2, 0, True)
            down(KT - 1, 1, False)
            for t in range(TT + 1):
                n = P if t < TT else B
                ve.wait_ge(y_squared, t + 1)
                ve.tensor_scalar(ms[0:n, t:t + 1], stat[0:n, 18 + t:19 + t], 1.0 / D, RMS_EPS, ALU.mult, ALU.add).then_inc(y_stat, 1)
                ve.wait_ge(y_root, t + 1)
                ve.reciprocal(rs[0:n, t:t + 1], rs[0:n, t:t + 1]).then_inc(y_inv, 1)
                ve.wait_ge(y_inv, t + 1)
                if t == 0:
                    ve.wait_ge(gf_in, 16)
                ve.scalar_tensor_tensor(out=y[0:n, t, :], in0=y[0:n, t, :], scalar=rs[0:n, t:t + 1], in1=gf_row[0:n, :],
                                        op0=ALU.mult, op1=ALU.mult).then_inc(y_done, 1)

        @block.tensor
        def _(pe):
            pe.wait_ge(ident_set, 2)
            pe.wait_ge(rows_in, 16 * 8)
            for k in range(KT):
                last = pe.transpose(psum[:, 3, k * NC:(k + 1) * NC], crow[:, k * P:(k + 1) * P], ident[0:NC, 0:NC])
            last.then_inc(cst_turned, 1)
            for t in range(TT + 1):
                n = P if t < TT else B
                base = 4 if t % 2 == 0 else 0
                for part, src in enumerate((x_tok[t], xn_tok[t])):
                    if part == 0:
                        pe.wait_ge(x_in[t], 16)
                        if t >= 2:
                            pe.wait_ge(xT_done, 2 * (t - 1))
                    else:
                        pe.wait_ge(xn_done, t + 1)
                        if t == 1:
                            pe.wait_ge(cst_done, 1)
                        if t >= 2:
                            pe.wait_ge(hg_done, 2 * (t - 1))
                    for k in range(KT):
                        last = pe.transpose(psum[:, base + 2 * part + k // 4, (k % 4) * P:(k % 4) * P + n],
                                            src[:, k * P:(k + 1) * P], ident[0:n, 0:n])
                    last.then_inc(x_turned, 1)

            def unit(g, s, rhs, t=None, dst=None, ks=range(KT), first=True, final=True, done=None):
                t = g if t is None else t
                dst = s if dst is None else dst
                if first:
                    pe.wait_ge(evicted, out_of(t - 2))
                pe.wait_ge(hi_done, g + 1)
                a = psum[:, 2 * (dst % 2):2 * (dst % 2) + 2, 0:H]
                for j, k in enumerate(ks):
                    if done is not None:
                        pe.wait_ge(done[0], done[1] + k)
                    for part in range(2):
                        for h in range(2):
                            pe.matmul(a[:, h, :], w_hi[:, s, j, :], rhs[:, 2 * k + part, h * H:(h + 1) * H],
                                      start=first and j == 0 and part == 0, stop=False)
                pe.wait_ge(lo_done, g + 1)
                for j, k in enumerate(ks):
                    for h in range(2):
                        last = pe.matmul(a[:, h, :], w_lo[:, s, j, :], rhs[:, 2 * k, h * H:(h + 1) * H],
                                         start=False, stop=final and j == len(ks) - 1)
                last.then_inc(mm_done, 1)

            def mean_over_features(src):
                for h in range(2):
                    last = pe.matmul(psum[:, 6 + h, 0:H], ones, src[:, h * H:(h + 1) * H], start=True, stop=True)
                return last

            pe.wait_ge(hg_done, 2 * (TT + 1))
            pe.wait_ge(xT_done, 2 * (TT + 1))
            pe.wait_ge(h_lo, 2 * (TT + 1))
            with pe.Fori(0, KT // 2) as it:
                for s in range(8):
                    unit(G_MIX + 8 * it + s, s % RING, act)

            pe.wait_ge(u_done, KT)
            pe.wait_ge(a_packed, 2)
            pe.wait_ge(tail_b_done, KT)
            tail = tail_b[:, :, :].rearrange("p r t -> p (r t)")
            for bank, src in ((5, a_pack[:, 0:SH]), (6, a_pack[:, SH:2 * SH]), (7, a_pack[:, 2 * SH:]), (4, tail)):
                pe.transpose(psum[0:src.shape[1], bank, 0:P], src, ident[:, :]).then_inc(a_turned, 1)
            pe.wait_ge(a_staged, 4)
            with pe.Fori(0, KT // RING) as it:
                for s in range(RING):
                    i = RING * it + s
                    unit(G_B + i, s, act)
                    pe.wait_ge(state_in, 16 * i + 16)
                    pe.wait_ge(win_done, 2 * i)
                    for h in range(2):
                        last = pe.transpose(psum[:, 4, h * SH:(h + 1) * SH], st_row[:, h, :], ident[0:SH, 0:SH])
                    last.then_inc(state_turned, 1)

            with pe.Fori(0, KT // RING) as it:
                for s in range(RING):
                    i = RING * it + s
                    unit(G_BOUT + i, s, mid, done=(act_lo, S_Q + 1))
            pe.wait_ge(vsum_done, KT)
            pe.wait_ge(sum_zero, 3)
            mean_over_features(vsum).then_inc(mean_done, 1)
            pe.wait_ge(frows_in, 32)
            pe.wait_ge(win_done, 2 * KT)
            for k in range(FT):
                last = pe.transpose(psum[:, 4, k * NCF:(k + 1) * NCF], frow[:, k * P:(k + 1) * P], ident[0:NCF, 0:NCF])
            last.then_inc(frow_turned, 1)

            with pe.Fori(0, 2) as it:
                for s in range(RING):
                    unit(G_GATE + RING * it + s, s, act)
            pe.wait_ge(ssum_done, KT)
            pe.wait_ge(centred, KT)
            mean_over_features(ssum).then_inc(var_done, 1)
            with pe.Fori(2, 4) as it:
                for s in range(RING):
                    unit(G_GATE + RING * it + s, s, act)

            for first, rhs, a in ((G_AOUT, mid, S_V), (G_O, act, S_M)):
                with pe.Fori(0, KT // RING) as it:
                    for s in range(RING):
                        unit(first + RING * it + s, s, rhs, done=(act_lo, a + 1))
            pe.wait_ge(ssum_done, 2 * KT)
            mean_over_features(ssum).then_inc(var_done, 1)

            with pe.Fori(0, FT // 2) as it:
                for s in range(RING):
                    unit(G_UP + RING * it + s, s, mid, done=(act_lo, S_H + 1))

            pe.wait_ge(fg_tail, FT)
            pe.wait_ge(cst_f_done, 1)
            nf, hb = PADB * FT, B // 2 * FT
            tail = cst[:, :, :].rearrange("p t c -> p (t c)")
            for j, (c, n) in enumerate(((0, nf), (nf, hb), (nf + hb, hb))):
                if j == 2:
                    pe.wait_ge(var_eps, 2)
                pe.transpose(psum[0:n, 4 + j, 0:P], tail[:, c:c + n], ident[:, :]).then_inc(f_turned, 1)

            def turn(n, par):
                pe.wait_ge(evicted, out_of(G_DOWN + n))
                src = (t0, t1)[par]
                for t in range(TT):
                    pe.transpose(psum[:, 4 + 2 * par, t * P:(t + 1) * P], src[:, t * P:(t + 1) * P], ident[:, :])
                pe.transpose(psum[0:B, 5 + 2 * par, 0:P], src[:, SEQ:N], ident[:, :]).then_inc(y_turned, 1)

            def down(n, par):
                for s in range(RING):
                    unit(G_DOWN + RING * n + s, s, act, t=G_DOWN + n, dst=par,
                         ks=range(KFIRST[s], KFIRST[s] + KSPLIT[s]), first=s == 0, final=s == RING - 1,
                         done=(act_lo, S_G + 1))

            pe.wait_ge(f_staged, 3)
            down(0, 0)
            with pe.Fori(0, KT // 2 - 1) as it:
                for par in range(2):
                    down(2 * it + 1 + par, 1 - par)
                    pe.wait_ge(y_copied, 4 * it)
                    turn(2 * it + par, par)
            down(KT - 1, 1)
            pe.wait_ge(y_copied, 2 * (KT - 2) - 2)
            turn(KT - 2, 0)
            pe.wait_ge(y_copied, 2 * (KT - 2))
            turn(KT - 1, 1)


_INS = ['x_prompt', 'x_sample', 'state_conv_a', 'state_conv_b', 'state_conv_ffn', 'g_mix', 'w_in', 'conv_a_w',
        'conv_a_b', 'ln_a_g', 'ln_a_b', 'w_a_out', 'conv_b_w', 'w_b_out', 'w_o', 'g_ffn', 'w_up', 'conv_f_w',
        'w_down', 'g_final']


def kernel(**inputs):
    import numpy as np
    import concourse.bacc as bacc
    from concourse import mybir as mb
    from concourse.bass_utils import run_bass_kernel_spmd

    nc = bacc.Bacc("TRN2", target_bir_lowering=False, num_devices=1)
    arrays, args = {}, []
    for name in _INS:
        a = np.ascontiguousarray(inputs[name])
        arrays[f"in_{name}"] = a
        args.append(nc.dram_tensor(f"in_{name}", a.shape, mb.dt.from_np(a.dtype), kind="ExternalInput").ap())
    batch, seq, d = inputs["x_prompt"].shape
    depth, dec, pad_a, d_a = inputs["state_conv_a"].shape
    _, _, pad_b, d_b = inputs["state_conv_b"].shape
    _, _, pad_f, d_ff = inputs["state_conv_ffn"].shape
    outs = [(batch, seq, d), tuple(inputs["x_sample"].shape), (depth, batch, pad_a, d_a), (depth, batch, pad_b, d_b),
            (depth, batch, pad_f, d_ff), (depth, dec, pad_a, d_a), (depth, dec, pad_b, d_b), (depth, dec, pad_f, d_ff)]
    for i, shape in enumerate(outs):
        args.append(nc.dram_tensor(f"out_{i}", shape, mb.dt.float32, kind="ExternalOutput").ap())
    build(nc, *args)
    r = run_bass_kernel_spmd(nc, [arrays], core_ids=[0])
    return tuple(r.results[0][f"out_{i}"] for i in range(len(outs)))
```

```python
from contextlib import ExitStack

import concourse.bass as bass
from concourse import mybir


P = 128
ALU = mybir.AluOpType
ACT = mybir.ActivationFunctionType
F32 = mybir.dt.float32
F32R = mybir.dt.float32r
X = mybir.AxisListType.X

RMS_EPS = 1e-6
LN_EPS = 1e-5
RING = 4
POOL_TAPS = 10
DVE_TAPS = (15, 2, 4)
START = 1


def build(nc, x_prompt, x_sample, state_a, state_b, state_f, g_mix, w_in, conv_a_w, conv_a_b, ln_a_g, ln_a_b,
          w_a_out, conv_b_w, w_b_out, w_o, g_ffn, w_up, conv_f_w, w_down, g_final,
          y_prompt, y_sample, a_prompt, b_prompt, f_prompt, a_sample, b_sample, f_sample):
    _, SEQ, D = x_prompt.shape
    B = x_sample.shape[0]
    WA, WB = conv_a_w.shape[1], conv_b_w.shape[1]
    FF = w_down.shape[1]
    KT = D // P
    FT = FF // P
    N = SEQ + B
    H = N // 2
    PADA, PADB = WA - 1, WB - 1
    TT = SEQ // P
    POOL_N, DVE_N = POOL_TAPS, sum(DVE_TAPS)
    TAP_CUTS = [sum(DVE_TAPS[:j]) for j in range(len(DVE_TAPS) + 1)]
    MIX_N = DVE_TAPS[0]
    assert POOL_N + DVE_N == WA
    assert KT == 8 and FT == 22 and WB == 3 and N % 4 == 0 and H <= 512

    C_WA, C_BA, C_LG, C_LB, C_GM, C_GF, C_WB = 0, WA, WA + 1, WA + 2, WA + 3, WA + 4, WA + 5
    C_SB = C_WB + WB
    NC = C_SB + B * PADB
    CF_W = B * PADB
    NCF = CF_W + WB

    G_MIX, G_B, G_BOUT, G_GATE, G_AOUT, G_O, G_UP = 0, 32, 40, 48, 64, 72, 80
    G_DOWN = G_UP + 2 * FT
    KSPLIT = (6, 6, 5, 5)
    KFIRST = (0, 6, 12, 17)
    S_Q, S_V, S_M, S_H, S_G = 0, 8, 16, 24, 32

    with ExitStack() as ctx:
        def sb(name, shape, dt=F32, stack=ctx):
            return stack.enter_context(nc.sbuf_tensor(name, shape, dt))

        def sem(name):
            return ctx.enter_context(nc.semaphore(name))

        ident = sb("ident", [P, P])
        cst = sb("cst", [P, KT, NC])
        tmp = sb("tmp", [P, 3, N])
        cx = sb("cx", [P, PADB + N])
        stat = sb("stat", [P, 24])
        raw = sb("raw", [P, RING, KT, P])
        w_hi = sb("w_hi", [P, RING, KT, P], F32R)
        w_lo = sb("w_lo", [P, RING, KT, P], F32R)
        xT = sb("xT", [P, KT, N])
        early = ExitStack()
        sb("act_tiles_0_to_7", [P, 2 * KT * N], F32R, early)
        v = sb("v", [P, KT, N], F32, early)
        gate_a = sb("gate_a", [P, KT, N], F32, early)
        y_b = sb("y_b", [P, KT, N], F32, early)
        UW = PADA + N
        u = sb("u", [P, KT, UW], F32, early)
        early.close()
        act = sb("act", [P, 2 * FT, N], F32R)
        FREE = KT * (3 * N + UW) - 2 * (FT - KT) * N
        sb("end_of_u", [P, FREE])
        middle = ExitStack()
        mid = sb("mid", [P, 2 * KT, N], F32R, middle)
        middle.close()
        final = ExitStack()
        y = sb("y", [P, TT + 1, D], F32, final)
        gf_row = sb("gf_row", [P, D], F32, final)
        sq_junk = sb("sq_junk", [P, D], F32, final)
        final.close()
        prods = sb("prods", [P, POOL_N - 1, SEQ])
        sb("mid_before_rows", [P, (TT + 3) * D - (POOL_N - 1) * SEQ])
        a_pack = sb("a_pack", [P, (PADA + B) * KT])
        tail_b = sb("tail_b", [P, PADB + B, KT])
        stage = sb("stage", [P, 4, P])
        assert (TT + 3) * D + (PADA + PADB + 2 * B) * KT + 4 * P <= 2 * KT * N and (TT + 3) * D >= (2 * KT - 3) * N

        psum = ctx.enter_context(nc.psum_tensor("psum", [P, 8, 512], F32))

        uf = u[:, :, :].rearrange("p t n -> p (t n)")
        tf = tmp[:, :, :].rearrange("p t n -> p (t n)")
        vf = v[:, :, :].rearrange("p t n -> p (t n)")
        gaf = gate_a[:, :, :].rearrange("p t n -> p (t n)")
        ybf = y_b[:, :, :].rearrange("p t n -> p (t n)")
        x_tok = [vf[:, t * D:(t + 1) * D] for t in range(TT)] + [ybf[0:B, D:2 * D]]
        xn_tok = [gaf[:, t * D:(t + 1) * D] for t in range(TT)] + [ybf[0:B, 2 * D:3 * D]]
        crow = ybf[0:NC, 0:D]
        u0 = KT * UW - FREE
        frow = uf[0:NCF, 0:FF]
        rinv = uf[:, u0:u0 + N]
        up_n = uf[:, u0 + N:u0 + 2 * N]
        cst_f = uf[:, u0 + 2 * N:u0 + 2 * N + FT * NCF].rearrange("p (t c) -> p t c", c=NCF)
        s2_at = u0 + 2 * N + FT * NCF
        ssum = uf[:, s2_at:s2_at + N]
        ones = uf[:, s2_at + N:s2_at + N + P]
        assert s2_at + N + P <= KT * UW and FF <= u0 + 2 * N
        tail_f = cst[:, :, :].rearrange("p t c -> p (t c)")[:, 0:(PADB + B) * FT].rearrange("p (r t) -> p r t", t=FT)
        t0, t1, t2 = (tmp[:, k, :] for k in range(3))
        win = t0[:, 0:B * WA].rearrange("p (b k) -> p b k", k=WA)
        win_w = t1[:, 0:B * WA].rearrange("p (b k) -> p b k", k=WA)
        SH = B * PADA // 2
        assert SH == PADA * KT // 2
        st_row = t1[0:SH, B * WA:B * WA + 2 * P].rearrange("p (h c) -> p h c", h=2)
        f_stage = [t2[:, j * P:(j + 1) * P] for j in range(3)]
        vsum = cx[:, 0:N]
        ms, rs = stat[:, 0:5], stat[:, 5:10]
        win_sum = stat[:, 10:18]

        x_in = [sem(f"x_in{t}") for t in range(TT + 1)]
        rows_in, frows_in, state_in, gf_in = sem("rows_in"), sem("frows_in"), sem("state_in"), sem("gf_in")
        raw_in = [sem(f"raw_in{s}") for s in range(RING)]
        const_set, ident_set = sem("const_set"), sem("ident_set")
        cst_turned, cst_done = sem("cst_turned"), sem("cst_done")
        x_squared, x_mean, x_root, x_inv, xn_done = (sem(n) for n in ("x_squared", "x_mean", "x_root", "x_inv", "xn_done"))
        x_turned, xT_done, hg_done, h_hi, h_lo = (sem(n) for n in ("x_turned", "xT_done", "hg_done", "h_hi", "h_lo"))
        hi_done, lo_done, mm_done, evicted = sem("hi_done"), sem("lo_done"), sem("mm_done"), sem("evicted")
        act_hi, act_lo, prod_done = sem("act_hi"), sem("act_lo"), sem("prod_done")
        u_done, prod_in, pool_sum, dve_tap, conv_b, tail_b_done = (sem(n) for n in ("u_done", "prod_in", "pool_sum", "dve_tap", "conv_b", "tail_b_done"))
        a_packed, a_turned, a_staged, state_turned, win_done, win_conv, v_done = (
            sem(n) for n in ("a_packed", "a_turned", "a_staged", "state_turned", "win_done", "win_conv", "v_done"))
        sum_zero, vsum_done, mean_done, frow_turned, cst_f_done = (
            sem(n) for n in ("sum_zero", "vsum_done", "mean_done", "frow_turned", "cst_f_done"))
        centred, squared, ssum_done, var_done, var_eps, var_root, rinv_done = (
            sem(n) for n in ("centred", "squared", "ssum_done", "var_done", "var_eps", "var_root", "rinv_done"))
        yb_gated, v_norm, v_sig, v_affine, table_set = (sem(n) for n in ("yb_gated", "v_norm", "v_sig", "v_affine", "table_set"))
        conv_f, fg_tail, silu_done = sem("conv_f"), sem("fg_tail"), sem("silu_done")
        f_turned, f_staged = sem("f_turned"), sem("f_staged")
        y_turned, y_copied, y_squared, y_stat, y_root, y_inv, y_done = (
            sem(n) for n in ("y_turned", "y_copied", "y_squared", "y_stat", "y_root", "y_inv", "y_done"))
        state_out = sem("state_out")
        y_out = sem("y_out")

        def out_of(t):
            return t + 3

        def summed(i, k):
            return (POOL_N - 1) * i + k + POOL_N

        def halves(ap):
            return ap.rearrange("p (a b) -> p a b", a=2)

        def tile(t, i, lo=0, hi=None):
            hi = t.shape[2] if hi is None else hi
            return t[:, bass.ds(i, 1), lo:hi].rearrange("p o n -> p (o n)")

        def scal(t, i, c):
            return t[:, bass.ds(i, 1), c:c + 1].rearrange("p o c -> p (o c)")

        def acc(s):
            return psum[:, 2 * (s % 2):2 * (s % 2) + 2, 0:H]

        stat_banks = psum[:, 6:8, 0:H]

        def kview(w, rows=None):
            w = w[0] if rows is None else w[0, rows[0]:rows[1], :]
            return w.rearrange("(k p) n -> p k n", p=P)

        wi = kview(w_in)
        COL = {"a_val": 0, "a_gate": D, "b_B": 2 * D, "b_C": 3 * D, "b_x": 4 * D, "g_A": 5 * D, "g_B": 6 * D}

        block = ctx.enter_context(nc.Block())

        @block.sync
        def _(sp):
            for t in range(TT):
                sp.dma_start(x_tok[t], x_prompt[0, t * P:(t + 1) * P, :]).then_inc(x_in[t], 16)
            sp.dma_start(x_tok[TT], x_sample.rearrange("b s d -> (b s) d")).then_inc(x_in[TT], 16)

            def load(g, s, src, k=KT):
                sp.wait_ge(lo_done, g - (RING - 1))
                sp.dma_start(raw[:, s, 0:k, :], src).then_inc(raw_in[s], 16)

            def pairs(first, names, w, it):
                for s in range(4):
                    c = names[s % 2] + (s // 2) * P + 2 * P * it
                    load(first + s, s, w[:, :, bass.ds(c, P)])

            for s in range(RING):
                c = (COL["a_val"], COL["a_gate"])[s % 2] + (s // 2) * P
                sp.dma_start(raw[:, s, :, :], wi[:, :, c:c + P]).then_inc(raw_in[s], 16)
            pairs(G_MIX + 4, (COL["b_C"], COL["b_x"]), wi, 0)
            with sp.Fori(1, KT // 2) as it:
                pairs(G_MIX + 8 * it, (COL["a_val"], COL["a_gate"]), wi, it)
                pairs(G_MIX + 8 * it + 4, (COL["b_C"], COL["b_x"]), wi, it)

            def plain(first, w, col):
                with sp.Fori(0, KT // RING) as it:
                    for s in range(RING):
                        load(first + RING * it + s, s, w[:, :, bass.ds(col + s * P + RING * P * it, P)])

            plain(G_B, wi, COL["b_B"])
            plain(G_BOUT, kview(w_b_out), 0)
            with sp.Fori(0, KT // 2) as it:
                pairs(G_GATE + 4 * it, (COL["g_A"], COL["g_B"]), wi, it)
            plain(G_AOUT, kview(w_a_out), 0)
            plain(G_O, kview(w_o), 0)
            wu = kview(w_up)
            with sp.Fori(0, FT // 2) as it:
                pairs(G_UP + 4 * it, (0, FF), wu, it)
            wd = kview(w_down)
            with sp.Fori(0, KT) as n:
                for s in range(RING):
                    load(G_DOWN + RING * n + s, s,
                         wd[:, KFIRST[s]:KFIRST[s] + KSPLIT[s], bass.ds(P * n, P)], KSPLIT[s])

            sp.wait_ge(mm_done, G_DOWN)
            sp.dma_start(gf_row[:, :], g_final.rearrange("(o d) -> o d", o=1).broadcast_to([P, D])).then_inc(gf_in, 16)
            for t in range(TT + 1):
                sp.wait_ge(y_done, t + 1)
                if t < TT:
                    sp.dma_start(y_prompt[0, t * P:(t + 1) * P, :], y[:, t, :]).then_inc(y_out, 16)
                else:
                    sp.dma_start(y_sample.rearrange("b s d -> (b s) d"), y[0:B, TT, :]).then_inc(y_out, 16)
            sp.wait_ge(y_out, 16 * (TT + 1))
            sp.wait_ge(state_out, 16 * 11)

        @block.gpsimd
        def _(pool):
            pool.sem_inc(pool_sum, summed(0, 0))
            pool.memset(ident[:, :], 0.0).then_inc(ident_set, 1)
            pool.wait_ge(ident_set, 1)
            pool.affine_select(out=ident[:, :], in_=ident[:, :], compare_op=ALU.not_equal, fill=1.0, base=0,
                               pattern=[[-1, P]], channel_multiplier=1).then_inc(ident_set, 1)
            pool.memset(u[:, :, 0:PADA], 0.0).then_inc(const_set, 1)
            pool.memset(cx[:, 0:PADB], 0.0).then_inc(const_set, 1)
            pool.wait_ge(const_set, 3)
            for i in range(KT):
                part = gate_a[:, i, 0:SEQ]
                for k in range(1, POOL_N):
                    pool.wait_ge(prod_in, POOL_N * i + k + 1)
                    pool.wait_ge(pool_sum, summed(i, k - 1))
                    pool.tensor_tensor(part, part, prods[:, k - 1, :], ALU.add).then_inc(pool_sum, 1)

        @block.scalar
        def _(sc):
            for started in (tail_b_done, win_done, fg_tail, silu_done, y_copied):
                sc.sem_inc(started, START)
            for r, n, src in ((C_WA, WA, conv_a_w[0]), (C_BA, 1, conv_a_b), (C_LG, 1, ln_a_g), (C_LB, 1, ln_a_b),
                              (C_GM, 1, g_mix), (C_GF, 1, g_ffn), (C_WB, WB, conv_b_w[0]),
                              (C_SB, B * PADB, state_b[0].rearrange("b k c -> (b k) c"))):
                sc.dma_start(crow[r:r + n, :], src).then_inc(rows_in, 16)
            for old, new in ((state_a, a_sample), (state_b, b_sample), (state_f, f_sample)):
                k = old.shape[2]
                sc.dma_start(new[0, :, 0:k - 1, :], old[0, :, 1:k, :]).then_inc(state_out, 16)

            def hi_split(g, s, k=KT, first=False):
                if first:
                    sc.wait_ge(raw_in[s], 16)
                else:
                    sc.wait_ge(raw_in[s], (g - s) * (16 // RING) + 16)
                    sc.wait_ge(mm_done, g - (RING - 1))
                sc.activation(w_hi[:, s, 0:k, :], raw[:, s, 0:k, :], ACT.Copy).then_inc(hi_done, 1)

            def evict(g, t, out, func):
                sc.wait_ge(mm_done, g + 1)
                sc.wait_ge(evicted, out_of(t - 1))
                sc.activation(halves(out), acc(g_slot[0]), func).then_inc(evicted, 1)

            g_slot = [0]

            def h_part(t):
                n = P if t < TT else B
                base = 4 if t % 2 == 0 else 0
                cols = slice(t * P, t * P + n)
                for b in range(2):
                    if b == 0:
                        sc.wait_ge(x_turned, 2 * t + 1)
                    sc.activation(xT[:, 4 * b:4 * b + 4, cols],
                                  psum[:, base + b, :].rearrange("p (k n) -> p k n", k=4)[:, :, 0:n],
                                  ACT.Copy).then_inc(xT_done, 1)
                for b in range(2):
                    sc.wait_ge(hg_done, 2 * t + b + 1)
                    hg = (t2 if b == 0 else cx[:, PADB:PADB + N])[:, 0:4 * n].rearrange("p (k n) -> p k n", k=4)
                    sc.activation(act[:, 8 * b:8 * b + 8:2, cols], hg, ACT.Copy).then_inc(h_hi, 1)

            sc.wait_ge(const_set, 3)
            for t in range(TT + 1):
                n = P if t < TT else B
                sc.wait_ge(x_in[t], 16)
                if t > 0:
                    sc.wait_ge(x_squared, t)
                sc.activation(tf[0:n, 0:D], x_tok[t], ACT.Square, accum_out=stat[0:n, 18 + t:19 + t]).then_inc(x_squared, 1)
                if t == 0:
                    sc.wait_ge(cst_turned, 1)
                    sc.activation(cst[:, :, :], psum[:, 3, 0:KT * NC].rearrange("p (t c) -> p t c", c=NC),
                                  ACT.Copy).then_inc(cst_done, 1)
                sc.wait_ge(x_mean, t + 1)
                sc.activation(rs[0:n, t:t + 1], ms[0:n, t:t + 1], ACT.Sqrt).then_inc(x_root, 1)
                if t > 0:
                    h_part(t - 1)
            h_part(TT)
            for s in range(RING):
                hi_split(s, s, first=True)
            sc.activation(rs, ms, ACT.Sigmoid).then_inc(table_set, 1)

            def products(i, first, last):
                for k in range(first, last):
                    if k == 0:
                        sc.wait_ge(u_done, START + i + 1)
                        out = tile(gate_a, i, 0, SEQ)
                    else:
                        sc.wait_ge(pool_sum, summed(i - 1, k))
                        out = prods[:, k - 1, :]
                    sc.activation(out, tile(u, i, k, k + SEQ), ACT.Copy, scale=scal(cst, i, C_WA + k)).then_inc(prod_in, 1)

            prod_cuts = {2: ((0, 0, 4),), 3: ((0, 4, 8),), 4: ((0, 8, POOL_N), (1, 0, 2)), 5: ((1, 2, 5),), 6: ((1, 5, 8),),
                         7: ((1, 8, POOL_N),)}
            with sc.Fori(0, KT // 2) as it:
                for s in range(8):
                    g = G_MIX + 8 * it + s
                    g_slot[0] = s
                    i = 2 * it + (s % 4) // 2
                    if s in (0, 2, 1, 3):
                        sc.wait_ge(u_done, START + i)
                        evict(g, g, t0 if s % 2 == 0 else t1, ACT.Copy if s % 2 == 0 else ACT.Sigmoid)
                    elif s % 2 == 0:
                        sc.wait_ge(u_done, START + 2 * it + 2)
                        evict(g, g, t0, ACT.Copy)
                    hi_split(g + RING, s % RING)
                    for odd, a, b in prod_cuts.get(s, ()):
                        products(2 * it + odd, a, b)
                    if s in (5, 7):
                        sc.wait_ge(evicted, out_of(g))
                        sc.activation(tail_b[:, :, bass.ds(i, 1)].rearrange("p r o -> p (r o)"), cx[:, SEQ:SEQ + PADB + B],
                                      ACT.Copy).then_inc(tail_b_done, 1)

            a_rows = a_prompt[0, 0].rearrange("r (t c) -> (r t) c", c=P)
            sc.wait_ge(u_done, START + KT)
            sc.dma_start(st_row, state_a[0].rearrange("b k c -> (b k) c")[:, 0:P].rearrange("(h p) c -> p h c", h=2)).then_inc(state_in, 16)
            for c, n, first in ((0, PADA, SEQ), (PADA * KT, B, PADA + SEQ)):
                sc.activation(a_pack[:, c:c + n * KT].rearrange("p (r t) -> p t r", t=KT), u[:, :, first:first + n],
                              ACT.Copy).then_inc(a_packed, 1)
            na, nb = SH, PADB * KT
            for j, n in enumerate((na, na, B * KT, nb + B * KT)):
                sc.wait_ge(a_turned, j + 1)
                sc.activation(stage[0:n, j, :], psum[0:n, (5, 6, 7, 4)[j], 0:P], ACT.Copy).then_inc(a_staged, 1)
            rows = lambda ap: ap.rearrange("r (t c) -> (r t) c", c=P)
            last_rows = lambda ap, k: ap[0, :, k - 1, :].rearrange("b (t c) -> b t c", c=P)
            for j, out, src in ((0, a_rows[0:na, :], stage[0:na, 0, :]), (1, a_rows[na:2 * na, :], stage[0:na, 1, :]),
                                (2, last_rows(a_sample, PADA), stage[0:B * KT, 2, :]),
                                (3, rows(b_prompt[0, 0]), stage[0:nb, 3, :]),
                                (3, last_rows(b_sample, PADB), stage[nb:nb + B * KT, 3, :])):
                sc.wait_ge(a_staged, j + 1)
                sc.dma_start(out, src).then_inc(state_out, 16)

            def state_tile(i, last=False):
                sc.wait_ge(state_turned, i + 1)
                sc.wait_ge(win_conv, START + 3 * i)
                sc.activation(win[:, :, 0:PADA], psum[:, 4, 0:B * PADA].rearrange("p (b k) -> p b k", k=PADA),
                              ACT.Copy).then_inc(win_done, 1)
                sc.activation(win[:, :, PADA:WA].rearrange("p b k -> p (b k)"), tile(u, i, PADA + SEQ, UW),
                              ACT.Copy).then_inc(win_done, 1)
                if not last:
                    src = state_a[0].rearrange("b k c -> (b k) c")[:, bass.ds(P * i + P, P)]
                    sc.dma_start(st_row, src.rearrange("(h p) c -> p h c", h=2)).then_inc(state_in, 16)

            def act_hi_split(out, src, sem_, value, scale=None):
                sc.wait_ge(sem_, value)
                if scale is None:
                    sc.activation(out, src, ACT.Copy).then_inc(act_hi, 1)
                else:
                    sc.activation(out, src, ACT.Copy, scale=scale).then_inc(act_hi, 1)

            def b_step(i, s, last=False):
                hi_split(G_B + RING + i, s)
                state_tile(i, last)
                sc.wait_ge(pool_sum, summed(KT - 1, POOL_N - 1))
                act_hi_split(tile(mid, 2 * i), t2, evicted, out_of(G_B + i))

            with sc.Fori(0, KT // RING - 1) as it:
                for s in range(RING):
                    b_step(RING * it + s, s)
            for s in range(RING):
                if s == 2:
                    sc.wait_ge(state_out, 16 * 8)
                b_step(KT - RING + s, s, last=s == RING - 1)

            with sc.Fori(0, KT // RING) as it:
                for s in range(RING):
                    g_slot[0] = s
                    i = RING * it + s
                    evict(G_BOUT + i, G_BOUT + i, tile(y_b, i), ACT.Copy)
                    hi_split(G_BOUT + RING + i, s)
            sc.wait_ge(v_done, KT)
            sc.wait_ge(win_done, START + 2 * KT)
            sc.dma_start(frow[0:CF_W, :], state_f[0].rearrange("b k c -> (b k) c")).then_inc(frows_in, 16)
            sc.dma_start(frow[CF_W:NCF, :], conv_f_w[0]).then_inc(frows_in, 16)
            sc.wait_ge(frow_turned, 1)
            sc.activation(cst_f, psum[:, 4, 0:FT * NCF].rearrange("p (t c) -> p t c", c=NCF), ACT.Copy).then_inc(cst_f_done, 1)

            def gate_step(it, s):
                g = G_GATE + RING * it + s
                g_slot[0] = s
                i = 2 * it + s // 2
                if s % 2 == 0:
                    evict(g, g, tile(gate_a, i), ACT.Sigmoid)
                else:
                    sc.wait_ge(yb_gated, START + i)
                    evict(g, g, t1, ACT.Sigmoid)
                hi_split(g + RING, s)

            with sc.Fori(0, 2) as it:
                for s in range(RING):
                    gate_step(it, s)
                    t = RING * it + s
                    sc.wait_ge(centred, t + 1)
                    sc.wait_ge(ssum_done, START + t)
                    sc.activation(t0, tile(v, t), ACT.Square).then_inc(squared, 1)
            sc.wait_ge(var_eps, 1)
            sc.activation(rinv, rinv, ACT.Sqrt).then_inc(var_root, 1)
            sc.activation(rs, ms, ACT.Sigmoid).then_inc(table_set, 1)
            with sc.Fori(2, 4) as it:
                for s in range(RING):
                    gate_step(it, s)
                    t = RING * it - 2 * RING + s
                    sc.wait_ge(v_norm, t + 1)
                    sc.wait_ge(prod_done, START + t)
                    sc.activation(t0, tile(v, t), ACT.Sigmoid, scale=scal(cst, t, C_LG),
                                  bias=scal(cst, t, C_LB)).then_inc(v_sig, 1)
                    sc.activation(tile(v, t), tile(v, t), ACT.Identity, scale=scal(cst, t, C_LG),
                                  bias=scal(cst, t, C_LB)).then_inc(v_affine, 1)
                    act_hi_split(tile(mid, 2 * t), t2, prod_done, START + t + 1)

            with sc.Fori(0, KT // RING) as it:
                for s in range(RING):
                    i = RING * it + s
                    hi_split(G_AOUT + RING + i, s)
                    act_hi_split(tile(act, 2 * i), t2, prod_done, START + KT + i + 1)

            with sc.Fori(0, KT // RING) as it:
                for s in range(RING):
                    i = RING * it + s
                    hi_split(G_O + RING + i, s)
                    sc.wait_ge(ssum_done, START + KT + i)
                    act_hi_split(tile(mid, 2 * i), tile(xT, i), evicted, out_of(G_O + i), scal(cst, i, C_GF))
                    sc.activation(t0, tile(xT, i), ACT.Square).then_inc(squared, 1)
            sc.wait_ge(var_eps, 2)
            sc.activation(rinv, rinv, ACT.Sqrt).then_inc(var_root, 1)
            sc.activation(rs, ms, ACT.Silu).then_inc(table_set, 1)

            with sc.Fori(0, FT // 2) as it:
                for s in range(RING):
                    g = G_UP + RING * it + s
                    i = 2 * it + s // 2
                    hi_split(g + RING, s)
                    if s % 2 == 0:
                        sc.wait_ge(evicted, out_of(g))
                        sc.activation(tail_f[:, :, bass.ds(i, 1)].rearrange("p r o -> p (r o)"),
                                      cx[:, SEQ:SEQ + PADB + B], ACT.Copy).then_inc(fg_tail, 1)
                        sc.wait_ge(conv_f, START + 6 * i + 6)
                        sc.wait_ge(prod_done, START + 2 * KT + i)
                        sc.activation(t1, t0, ACT.Silu).then_inc(silu_done, 1)
                    else:
                        act_hi_split(tile(act, 2 * i), t2, prod_done, START + 2 * KT + i + 1)

            nf, hb = PADB * FT, B // 2
            sc.wait_ge(act_lo, START + S_G + FT)
            for j in range(3):
                sc.wait_ge(f_turned, j + 1)
                n = nf if j == 0 else hb * FT
                sc.activation(f_stage[j][0:n, :], psum[0:n, 4 + j, 0:P], ACT.Copy).then_inc(f_staged, 1)
                sc.wait_ge(f_staged, j + 1)
                if j == 0:
                    sc.dma_start(f_prompt[0, 0].rearrange("r (t c) -> (r t) c", c=P), f_stage[j][0:n, :]).then_inc(state_out, 16)
                else:
                    sc.dma_start(f_sample[0, (j - 1) * hb:j * hb, PADB - 1, :].rearrange("b (t c) -> b t c", c=P),
                                 f_stage[j][0:n, :]).then_inc(state_out, 16)
            sc.activation(rs, ms, ACT.Sqrt).then_inc(table_set, 1)

            def y_tile(n, par):
                sc.wait_ge(y_turned, START + n + 1)
                main = psum[:, 4 + 2 * par, :].rearrange("p (t c) -> p t c", c=P)
                side = psum[0:B, 5 + 2 * par, 0:P]
                sc.activation(y[:, 0:TT, bass.ds(P * n, P)], main, ACT.Copy).then_inc(y_copied, 1)
                sc.activation(y[0:B, TT, bass.ds(P * n, P)], side, ACT.Copy).then_inc(y_copied, 1)

            def down_split(n, s):
                hi_split(G_DOWN + RING * n + RING + s, s, KSPLIT[s])

            with sc.Fori(0, KT // 2 - 1) as it:
                for par in range(2):
                    for s in range(RING):
                        down_split(2 * it + par, s)
                    y_tile(2 * it + par, par)
            for s in range(RING):
                down_split(KT - 2, s)
            y_tile(KT - 2, 0)
            y_tile(KT - 1, 1)
            for t in range(TT + 1):
                n = P if t < TT else B
                sc.wait_ge(y_copied, START + 2 * KT)
                if t > 0:
                    sc.wait_ge(y_squared, t)
                sc.activation(sq_junk[0:n, :], y[0:n, t, :], ACT.Square, accum_out=stat[0:n, 18 + t:19 + t]).then_inc(y_squared, 1)
                sc.wait_ge(y_stat, t + 1)
                sc.activation(rs[0:n, t:t + 1], ms[0:n, t:t + 1], ACT.Sqrt).then_inc(y_root, 1)

        @block.vector
        def _(ve):
            for started in (u_done, conv_b, win_conv, vsum_done, ssum_done, yb_gated, prod_done, conv_f, act_lo):
                ve.sem_inc(started, START)
            ve.sem_inc(evicted, out_of(-1))
            ve.memset(stat[:, :], 1.0).then_inc(const_set, 1)

            def lo_split(g, s, k=KT, first=False):
                ve.wait_ge(hi_done, g + 1)
                if not first:
                    ve.wait_ge(mm_done, g - (RING - 1))
                ve.tensor_tensor(w_lo[:, s, 0:k, :], raw[:, s, 0:k, :], w_hi[:, s, 0:k, :], ALU.subtract).then_inc(lo_done, 1)

            def act_lo_split(out, src, hi, a):
                ve.wait_ge(act_hi, a + 1)
                ve.tensor_tensor(out, src, hi, ALU.subtract).then_inc(act_lo, 1)

            def out_of_psum(g, t):
                ve.wait_ge(mm_done, g + 1)
                ve.wait_ge(evicted, out_of(t - 1))

            def h_part(t):
                n = P if t < TT else B
                base = 6 if t % 2 == 0 else 2
                cols = slice(t * P, t * P + n)
                ve.wait_ge(x_turned, 2 * t + 2)
                for b in range(2):
                    if t > 0:
                        ve.wait_ge(h_lo, 2 * t - 1 + b)
                    hg = (t2 if b == 0 else cx[:, PADB:PADB + N])[:, 0:4 * n].rearrange("p (k n) -> p k n", k=4)
                    g = cst[:, 4 * b:4 * b + 4, C_GM:C_GM + 1].broadcast_to([P, 4, n])
                    ve.tensor_tensor(hg, psum[:, base + b, :].rearrange("p (k n) -> p k n", k=4)[:, :, 0:n], g,
                                     ALU.mult).then_inc(hg_done, 1)
                for b in range(2):
                    ve.wait_ge(h_hi, 2 * t + b + 1)
                    hg = (t2 if b == 0 else cx[:, PADB:PADB + N])[:, 0:4 * n].rearrange("p (k n) -> p k n", k=4)
                    ve.tensor_tensor(act[:, 8 * b + 1:8 * b + 8:2, cols], hg, act[:, 8 * b:8 * b + 8:2, cols],
                                     ALU.subtract).then_inc(h_lo, 1)

            for t in range(TT + 1):
                n = P if t < TT else B
                ve.wait_ge(x_squared, t + 1)
                ve.tensor_scalar(ms[0:n, t:t + 1], stat[0:n, 18 + t:19 + t], 1.0 / D, RMS_EPS, ALU.mult, ALU.add).then_inc(x_mean, 1)
                ve.wait_ge(x_root, t + 1)
                ve.reciprocal(rs[0:n, t:t + 1], rs[0:n, t:t + 1]).then_inc(x_inv, 1)
                ve.wait_ge(x_inv, t + 1)
                ve.tensor_scalar(xn_tok[t], x_tok[t], rs[0:n, t:t + 1], None, ALU.mult).then_inc(xn_done, 1)
                if t == 0:
                    ve.wait_ge(cst_done, 1)
                    ve.wait_ge(const_set, 3)
                else:
                    h_part(t - 1)
            h_part(TT)
            for s in range(RING):
                lo_split(s, s, first=True)

            def taps(i, first, last):
                for k in range(first, last):
                    src, w = tile(u, i, POOL_N + k, POOL_N + k + SEQ), scal(cst, i, C_WA + POOL_N + k)
                    out = tile(v, i, 0, SEQ)
                    if k == 0:
                        ve.wait_ge(u_done, START + i + 1)
                        ve.tensor_scalar(out, src, w, scal(cst, i, C_BA), ALU.mult, ALU.add).then_inc(dve_tap, 1)
                        continue
                    group = max(j for j in range(len(DVE_TAPS)) if TAP_CUTS[j] <= k)
                    if k > TAP_CUTS[group]:
                        ve.wait_ge(dve_tap, KT * TAP_CUTS[group] + DVE_TAPS[group] * i + k - TAP_CUTS[group])
                    ve.scalar_tensor_tensor(out=out, in0=src, scalar=w, in1=out, op0=ALU.mult,
                                            op1=ALU.add).then_inc(dve_tap, 1)

            def narrow(i, out_main, out_side, w, w_c, state, s_c, done):
                for k in range(WB):
                    wk = scal(w, i, w_c + k)
                    side = cx[:, PADB + SEQ:PADB + N] if k == PADB else \
                        state[:, bass.ds(i, 1), s_c + k:s_c + B * PADB:PADB].rearrange("p o b -> p (o b)")
                    for j, (out, src) in enumerate(((out_main, cx[:, k:k + SEQ]), (out_side, side))):
                        if k == 0:
                            ve.tensor_scalar(out, src, wk, None, ALU.mult).then_inc(done, 1)
                        else:
                            ve.wait_ge(done, START + 6 * i + 2 * k + j - 1)
                            ve.scalar_tensor_tensor(out=out, in0=src, scalar=wk, in1=out, op0=ALU.mult,
                                                    op1=ALU.add).then_inc(done, 1)

            cuts = {1: ((0, 0, 5),), 2: ((0, 5, 11),), 3: ((0, 11, MIX_N), (1, 0, 1)), 4: ((1, 1, 7),), 5: ((1, 7, 8),),
                    6: ((1, 8, MIX_N - 1),), 7: ((1, MIX_N - 1, MIX_N),)}
            with ve.Fori(0, KT // 2) as it:
                for s in range(8):
                    g = G_MIX + 8 * it + s
                    i = 2 * it + (s % 4) // 2
                    if s in (1, 3):
                        ve.wait_ge(evicted, out_of(g))
                        ve.tensor_tensor(tile(u, i, PADA, UW), t0, t1, ALU.mult).then_inc(u_done, 1)
                    if s in (5, 7):
                        out_of_psum(g, g)
                        ve.wait_ge(tail_b_done, START + i)
                        ve.wait_ge(conv_b, START + 6 * i)
                        ve.tensor_tensor(halves(cx[:, PADB:PADB + N]), acc(s), halves(t0), ALU.mult).then_inc(evicted, 1)
                    lo_split(g + RING, s % RING)
                    if s in (5, 7):
                        ve.wait_ge(evicted, out_of(g))
                        narrow(i, tile(y_b, i, 0, SEQ), tile(y_b, i, SEQ, N), cst, C_WB, cst, C_SB, conv_b)
                    for odd, a, b in cuts.get(s, ()):
                        taps(2 * it + odd, a, b)

            ve.wait_ge(dve_tap, KT * TAP_CUTS[1])
            with ve.Fori(0, KT // RING) as it:
                for s in range(RING):
                    i = RING * it + s
                    out_of_psum(G_B + i, G_B + i)
                    ve.wait_ge(act_lo, START + i)
                    ve.wait_ge(conv_b, START + 6 * KT)
                    ve.tensor_tensor(halves(t2), acc(s), halves(tile(y_b, i)), ALU.mult).then_inc(evicted, 1)
                    lo_split(G_B + RING + i, s)
                    ve.wait_ge(win_done, START + 2 * i + 2)
                    wa = cst[:, bass.ds(i, 1), C_WA:C_WA + WA].broadcast_to([P, B, WA])
                    ve.tensor_tensor(win_w, win, wa, ALU.mult).then_inc(win_conv, 1)
                    ve.wait_ge(win_conv, START + 3 * i + 1)
                    ve.tensor_reduce(win_sum, win_w, X, ALU.add).then_inc(win_conv, 1)
                    act_lo_split(tile(mid, 2 * i + 1), t2, tile(mid, 2 * i), S_Q + i)
                    taps(i, TAP_CUTS[1], TAP_CUTS[2])
                    ve.wait_ge(win_conv, START + 3 * i + 2)
                    ve.tensor_scalar(tile(v, i, SEQ, N), win_sum, scal(cst, i, C_BA), None, ALU.add).then_inc(win_conv, 1)

            ve.wait_ge(tail_b_done, START + KT)
            ve.memset(vsum, 0.0).then_inc(sum_zero, 1)
            ve.wait_ge(sum_zero, 1)
            ve.wait_ge(dve_tap, KT * TAP_CUTS[2])
            ve.wait_ge(win_conv, START + 3 * KT)
            with ve.Fori(0, KT // RING) as it:
                for s in range(RING):
                    i = RING * it + s
                    taps(i, TAP_CUTS[2], DVE_N)
                    lo_split(G_BOUT + RING + i, s)
                    ve.wait_ge(pool_sum, summed(i, POOL_N - 1))
                    ve.wait_ge(dve_tap, KT * TAP_CUTS[2] + DVE_TAPS[2] * (i + 1))
                    ve.tensor_tensor(tile(v, i, 0, SEQ), tile(v, i, 0, SEQ), tile(gate_a, i, 0, SEQ), ALU.add).then_inc(v_done, 1)
                    ve.wait_ge(v_done, i + 1)
                    ve.wait_ge(vsum_done, START + i)
                    ve.tensor_tensor(vsum, vsum, tile(v, i), ALU.add).then_inc(vsum_done, 1)
            ve.memset(ones, 1.0 / D).then_inc(sum_zero, 1)
            ve.memset(ssum, 0.0).then_inc(sum_zero, 1)
            ve.wait_ge(sum_zero, 3)

            def gate_step(it, s):
                g = G_GATE + RING * it + s
                if s % 2 == 1:
                    i = 2 * it + s // 2
                    ve.wait_ge(evicted, out_of(g))
                    ve.tensor_tensor(tile(y_b, i), tile(y_b, i), t1, ALU.mult).then_inc(yb_gated, 1)
                lo_split(g + RING, s)

            def square_sum(t, at):
                ve.wait_ge(squared, at + t + 1)
                ve.wait_ge(ssum_done, START + at + t)
                ve.tensor_tensor(ssum, ssum, t0, ALU.add).then_inc(ssum_done, 1)

            def root(n, eps):
                ve.wait_ge(var_done, n)
                ve.tensor_scalar(halves(rinv), stat_banks, eps, None, ALU.add).then_inc(var_eps, 1)
                ve.wait_ge(var_root, n)
                ve.reciprocal(rinv, rinv).then_inc(rinv_done, 1)
                ve.wait_ge(rinv_done, n)

            ve.wait_ge(mean_done, 1)
            with ve.Fori(0, 2) as it:
                for s in range(RING):
                    t = RING * it + s
                    ve.tensor_tensor(halves(tile(v, t)), halves(tile(v, t)), stat_banks, ALU.subtract).then_inc(centred, 1)
                    gate_step(it, s)
                    square_sum(t, 0)
            ve.wait_ge(frow_turned, 1)
            root(1, LN_EPS)
            ve.memset(ssum, 0.0).then_inc(sum_zero, 1)
            with ve.Fori(2, 4) as it:
                for s in range(RING):
                    t = RING * it - 2 * RING + s
                    ve.wait_ge(centred, KT)
                    ve.tensor_tensor(tile(v, t), tile(v, t), rinv, ALU.mult).then_inc(v_norm, 1)
                    gate_step(it, s)
                    ve.wait_ge(v_affine, t + 1)
                    ve.wait_ge(act_lo, START + S_V + t)
                    ve.tensor_tensor(t2, tile(v, t), t0, ALU.mult).then_inc(prod_done, 1)
                    act_lo_split(tile(mid, 2 * t + 1), t2, tile(mid, 2 * t), S_V + t)

            ve.wait_ge(yb_gated, START + KT)
            with ve.Fori(0, KT // RING) as it:
                for s in range(RING):
                    i = RING * it + s
                    g = G_AOUT + i
                    out_of_psum(g, g)
                    ve.wait_ge(prod_done, START + KT + i)
                    ve.tensor_tensor(halves(t1), acc(s), halves(tile(gate_a, i)), ALU.mult).then_inc(evicted, 1)
                    ve.wait_ge(evicted, out_of(g))
                    ve.wait_ge(act_lo, START + S_M + i)
                    ve.tensor_tensor(t2, t1, tile(y_b, i), ALU.add).then_inc(prod_done, 1)
                    lo_split(g + RING, s)
                    act_lo_split(tile(act, 2 * i + 1), t2, tile(act, 2 * i), S_M + i)

            ve.wait_ge(sum_zero, 4)
            with ve.Fori(0, KT // RING) as it:
                for s in range(RING):
                    i = RING * it + s
                    g = G_O + i
                    out_of_psum(g, g)
                    ve.tensor_tensor(halves(tile(xT, i)), acc(s), halves(tile(xT, i)), ALU.add).then_inc(evicted, 1)
                    lo_split(g + RING, s)
                    ve.wait_ge(act_hi, S_H + i + 1)
                    ve.wait_ge(evicted, out_of(g))
                    ve.scalar_tensor_tensor(out=tile(mid, 2 * i + 1), in0=tile(xT, i), scalar=scal(cst, i, C_GF),
                                            in1=tile(mid, 2 * i), op0=ALU.mult, op1=ALU.subtract).then_inc(act_lo, 1)
                    square_sum(i, KT)
            root(2, RMS_EPS)
            ve.memset(cx[:, 0:PADB], 0.0).then_inc(sum_zero, 1)
            ve.wait_ge(sum_zero, 5)
            ve.wait_ge(cst_f_done, 1)

            with ve.Fori(0, FT // 2) as it:
                for s in range(RING):
                    g = G_UP + RING * it + s
                    i = 2 * it + s // 2
                    out_of_psum(g, g)
                    if s % 2 == 0:
                        ve.wait_ge(fg_tail, START + i)
                        ve.wait_ge(conv_f, START + 6 * i)
                        ve.wait_ge(silu_done, START + i)
                        ve.tensor_tensor(halves(cx[:, PADB:PADB + N]), acc(s), halves(rinv), ALU.mult).then_inc(evicted, 1)
                        ve.wait_ge(evicted, out_of(g))
                        narrow(i, t0[:, 0:SEQ], t0[:, SEQ:N], cst_f, CF_W, cst_f, 0, conv_f)
                        lo_split(g + RING, s)
                    else:
                        ve.tensor_tensor(halves(up_n), acc(s), halves(rinv), ALU.mult).then_inc(evicted, 1)
                        ve.wait_ge(evicted, out_of(g))
                        ve.wait_ge(silu_done, START + i + 1)
                        ve.wait_ge(act_lo, START + S_G + i)
                        ve.tensor_tensor(t2, up_n, t1, ALU.mult).then_inc(prod_done, 1)
                        lo_split(g + RING, s)
                        act_lo_split(tile(act, 2 * i + 1), t2, tile(act, 2 * i), S_G + i)

            def down(n, par, split):
                if split:
                    for s in range(RING):
                        lo_split(G_DOWN + RING * n + RING + s, s, KSPLIT[s])
                ve.wait_ge(mm_done, G_DOWN + RING * n + RING)
                ve.wait_ge(evicted, out_of(G_DOWN + n - 1))
                ve.wait_ge(y_turned, START + n)
                out = (t0, t1)[par]
                ve.tensor_tensor(halves(out), acc(par), halves(tile(xT, n)), ALU.add).then_inc(evicted, 1)

            with ve.Fori(0, KT // 2 - 1) as it:
                for par in range(2):
                    down(2 * it + par, par, True)
            down(KT - 2, 0, True)
            down(KT - 1, 1, False)
            for t in range(TT + 1):
                n = P if t < TT else B
                ve.wait_ge(y_squared, t + 1)
                ve.tensor_scalar(ms[0:n, t:t + 1], stat[0:n, 18 + t:19 + t], 1.0 / D, RMS_EPS, ALU.mult, ALU.add).then_inc(y_stat, 1)
                ve.wait_ge(y_root, t + 1)
                ve.reciprocal(rs[0:n, t:t + 1], rs[0:n, t:t + 1]).then_inc(y_inv, 1)
                ve.wait_ge(y_inv, t + 1)
                if t == 0:
                    ve.wait_ge(gf_in, 16)
                ve.scalar_tensor_tensor(out=y[0:n, t, :], in0=y[0:n, t, :], scalar=rs[0:n, t:t + 1], in1=gf_row[0:n, :],
                                        op0=ALU.mult, op1=ALU.mult).then_inc(y_done, 1)

        @block.tensor
        def _(pe):
            pe.sem_inc(y_turned, START)
            pe.wait_ge(ident_set, 2)
            pe.wait_ge(rows_in, 16 * 8)
            for k in range(KT):
                last = pe.transpose(psum[:, 3, k * NC:(k + 1) * NC], crow[:, k * P:(k + 1) * P], ident[0:NC, 0:NC])
            last.then_inc(cst_turned, 1)
            for t in range(TT + 1):
                n = P if t < TT else B
                base = 4 if t % 2 == 0 else 0
                for part, src in enumerate((x_tok[t], xn_tok[t])):
                    if part == 0:
                        pe.wait_ge(x_in[t], 16)
                        if t >= 2:
                            pe.wait_ge(xT_done, 2 * (t - 1))
                    else:
                        pe.wait_ge(xn_done, t + 1)
                        if t == 1:
                            pe.wait_ge(cst_done, 1)
                        if t >= 2:
                            pe.wait_ge(hg_done, 2 * (t - 1))
                    for k in range(KT):
                        last = pe.transpose(psum[:, base + 2 * part + k // 4, (k % 4) * P:(k % 4) * P + n],
                                            src[:, k * P:(k + 1) * P], ident[0:n, 0:n])
                    last.then_inc(x_turned, 1)

            def unit(g, s, rhs, t=None, dst=None, ks=range(KT), first=True, final=True, done=None):
                t = g if t is None else t
                dst = s if dst is None else dst
                if first:
                    pe.wait_ge(evicted, out_of(t - 2))
                pe.wait_ge(hi_done, g + 1)
                a = psum[:, 2 * (dst % 2):2 * (dst % 2) + 2, 0:H]
                for j, k in enumerate(ks):
                    if done is not None:
                        pe.wait_ge(done[0], START + done[1] + k)
                    for part in range(2):
                        for h in range(2):
                            pe.matmul(a[:, h, :], w_hi[:, s, j, :], rhs[:, 2 * k + part, h * H:(h + 1) * H],
                                      start=first and j == 0 and part == 0, stop=False)
                pe.wait_ge(lo_done, g + 1)
                for j, k in enumerate(ks):
                    for h in range(2):
                        last = pe.matmul(a[:, h, :], w_lo[:, s, j, :], rhs[:, 2 * k, h * H:(h + 1) * H],
                                         start=False, stop=final and j == len(ks) - 1)
                last.then_inc(mm_done, 1)

            def mean_over_features(src):
                for h in range(2):
                    last = pe.matmul(psum[:, 6 + h, 0:H], ones, src[:, h * H:(h + 1) * H], start=True, stop=True)
                return last

            pe.wait_ge(hg_done, 2 * (TT + 1))
            pe.wait_ge(xT_done, 2 * (TT + 1))
            pe.wait_ge(h_lo, 2 * (TT + 1))
            with pe.Fori(0, KT // 2) as it:
                for s in range(8):
                    unit(G_MIX + 8 * it + s, s % RING, act)

            pe.wait_ge(u_done, START + KT)
            pe.wait_ge(a_packed, 2)
            pe.wait_ge(tail_b_done, START + KT)
            tail = tail_b[:, :, :].rearrange("p r t -> p (r t)")
            for bank, src in ((5, a_pack[:, 0:SH]), (6, a_pack[:, SH:2 * SH]), (7, a_pack[:, 2 * SH:]), (4, tail)):
                pe.transpose(psum[0:src.shape[1], bank, 0:P], src, ident[:, :]).then_inc(a_turned, 1)
            pe.wait_ge(a_staged, 4)
            with pe.Fori(0, KT // RING) as it:
                for s in range(RING):
                    i = RING * it + s
                    unit(G_B + i, s, act)
                    pe.wait_ge(state_in, 16 * i + 16)
                    pe.wait_ge(win_done, START + 2 * i)
                    for h in range(2):
                        last = pe.transpose(psum[:, 4, h * SH:(h + 1) * SH], st_row[:, h, :], ident[0:SH, 0:SH])
                    last.then_inc(state_turned, 1)

            with pe.Fori(0, KT // RING) as it:
                for s in range(RING):
                    i = RING * it + s
                    unit(G_BOUT + i, s, mid, done=(act_lo, S_Q + 1))
            pe.wait_ge(vsum_done, START + KT)
            pe.wait_ge(sum_zero, 3)
            mean_over_features(vsum).then_inc(mean_done, 1)
            pe.wait_ge(frows_in, 32)
            pe.wait_ge(win_done, START + 2 * KT)
            for k in range(FT):
                last = pe.transpose(psum[:, 4, k * NCF:(k + 1) * NCF], frow[:, k * P:(k + 1) * P], ident[0:NCF, 0:NCF])
            last.then_inc(frow_turned, 1)

            with pe.Fori(0, 2) as it:
                for s in range(RING):
                    unit(G_GATE + RING * it + s, s, act)
            pe.wait_ge(ssum_done, START + KT)
            pe.wait_ge(centred, KT)
            mean_over_features(ssum).then_inc(var_done, 1)
            with pe.Fori(2, 4) as it:
                for s in range(RING):
                    unit(G_GATE + RING * it + s, s, act)

            for first, rhs, a in ((G_AOUT, mid, S_V), (G_O, act, S_M)):
                with pe.Fori(0, KT // RING) as it:
                    for s in range(RING):
                        unit(first + RING * it + s, s, rhs, done=(act_lo, a + 1))
            pe.wait_ge(ssum_done, START + 2 * KT)
            mean_over_features(ssum).then_inc(var_done, 1)

            with pe.Fori(0, FT // 2) as it:
                for s in range(RING):
                    unit(G_UP + RING * it + s, s, mid, done=(act_lo, S_H + 1))

            pe.wait_ge(fg_tail, START + FT)
            pe.wait_ge(cst_f_done, 1)
            nf, hb = PADB * FT, B // 2 * FT
            tail = cst[:, :, :].rearrange("p t c -> p (t c)")
            for j, (c, n) in enumerate(((0, nf), (nf, hb), (nf + hb, hb))):
                if j == 2:
                    pe.wait_ge(var_eps, 2)
                pe.transpose(psum[0:n, 4 + j, 0:P], tail[:, c:c + n], ident[:, :]).then_inc(f_turned, 1)

            def turn(n, par):
                pe.wait_ge(evicted, out_of(G_DOWN + n))
                src = (t0, t1)[par]
                for t in range(TT):
                    pe.transpose(psum[:, 4 + 2 * par, t * P:(t + 1) * P], src[:, t * P:(t + 1) * P], ident[:, :])
                pe.transpose(psum[0:B, 5 + 2 * par, 0:P], src[:, SEQ:N], ident[:, :]).then_inc(y_turned, 1)

            def down(n, par):
                for s in range(RING):
                    unit(G_DOWN + RING * n + s, s, act, t=G_DOWN + n, dst=par,
                         ks=range(KFIRST[s], KFIRST[s] + KSPLIT[s]), first=s == 0, final=s == RING - 1,
                         done=(act_lo, S_G + 1))

            pe.wait_ge(f_staged, 3)
            down(0, 0)
            with pe.Fori(0, KT // 2 - 1) as it:
                for par in range(2):
                    down(2 * it + 1 + par, 1 - par)
                    pe.wait_ge(y_copied, START + 4 * it)
                    turn(2 * it + par, par)
            down(KT - 1, 1)
            pe.wait_ge(y_copied, START + 2 * (KT - 2) - 2)
            turn(KT - 2, 0)
            pe.wait_ge(y_copied, START + 2 * (KT - 2))
            turn(KT - 1, 1)


_INS = ['x_prompt', 'x_sample', 'state_conv_a', 'state_conv_b', 'state_conv_ffn', 'g_mix', 'w_in', 'conv_a_w',
        'conv_a_b', 'ln_a_g', 'ln_a_b', 'w_a_out', 'conv_b_w', 'w_b_out', 'w_o', 'g_ffn', 'w_up', 'conv_f_w',
        'w_down', 'g_final']


def kernel(**inputs):
    import numpy as np
    import concourse.bacc as bacc
    from concourse import mybir as mb
    from concourse.bass_utils import run_bass_kernel_spmd

    nc = bacc.Bacc("TRN2", target_bir_lowering=False, num_devices=1)
    arrays, args = {}, []
    for name in _INS:
        a = np.ascontiguousarray(inputs[name])
        arrays[f"in_{name}"] = a
        args.append(nc.dram_tensor(f"in_{name}", a.shape, mb.dt.from_np(a.dtype), kind="ExternalInput").ap())
    batch, seq, d = inputs["x_prompt"].shape
    depth, dec, pad_a, d_a = inputs["state_conv_a"].shape
    _, _, pad_b, d_b = inputs["state_conv_b"].shape
    _, _, pad_f, d_ff = inputs["state_conv_ffn"].shape
    outs = [(batch, seq, d), tuple(inputs["x_sample"].shape), (depth, batch, pad_a, d_a), (depth, batch, pad_b, d_b),
            (depth, batch, pad_f, d_ff), (depth, dec, pad_a, d_a), (depth, dec, pad_b, d_b), (depth, dec, pad_f, d_ff)]
    for i, shape in enumerate(outs):
        args.append(nc.dram_tensor(f"out_{i}", shape, mb.dt.float32, kind="ExternalOutput").ap())
    build(nc, *args)
    r = run_bass_kernel_spmd(nc, [arrays], core_ids=[0])
    return tuple(r.results[0][f"out_{i}"] for i in range(len(outs)))
```

```python
from contextlib import ExitStack

import concourse.bass as bass
from concourse import mybir


P = 128
ALU = mybir.AluOpType
ACT = mybir.ActivationFunctionType
F32 = mybir.dt.float32
F32R = mybir.dt.float32r
X = mybir.AxisListType.X

RMS_EPS = 1e-6
LN_EPS = 1e-5
RING = 4
POOL_TAPS = 10
DVE_TAPS = (15, 2, 4)
START = 1


def build(nc, x_prompt, x_sample, state_a, state_b, state_f, g_mix, w_in, conv_a_w, conv_a_b, ln_a_g, ln_a_b,
          w_a_out, conv_b_w, w_b_out, w_o, g_ffn, w_up, conv_f_w, w_down, g_final,
          y_prompt, y_sample, a_prompt, b_prompt, f_prompt, a_sample, b_sample, f_sample):
    _, SEQ, D = x_prompt.shape
    B = x_sample.shape[0]
    WA, WB = conv_a_w.shape[1], conv_b_w.shape[1]
    FF = w_down.shape[1]
    KT = D // P
    FT = FF // P
    N = SEQ + B
    H = N // 2
    PADA, PADB = WA - 1, WB - 1
    TT = SEQ // P
    POOL_N, DVE_N = POOL_TAPS, sum(DVE_TAPS)
    TAP_CUTS = [sum(DVE_TAPS[:j]) for j in range(len(DVE_TAPS) + 1)]
    MIX_N = DVE_TAPS[0]
    assert POOL_N + DVE_N == WA
    assert KT == 8 and FT == 22 and WB == 3 and N % 4 == 0 and H <= 512

    C_WA, C_BA, C_LG, C_LB, C_GM, C_GF, C_WB = 0, WA, WA + 1, WA + 2, WA + 3, WA + 4, WA + 5
    C_SB = C_WB + WB
    NC = C_SB + B * PADB
    CF_W = B * PADB
    NCF = CF_W + WB

    G_MIX, G_B, G_BOUT, G_GATE, G_AOUT, G_O, G_UP = 0, 32, 40, 48, 64, 72, 80
    G_DOWN = G_UP + 2 * FT
    KSPLIT = (6, 6, 5, 5)
    KFIRST = (0, 6, 12, 17)
    S_Q, S_V, S_M, S_H, S_G = 0, 8, 16, 24, 32
    SQUARE_STEPS = {2 + j: (2 * j, 2 * j + 1) for j in range(KT // 2)}
    ROOT_STEP = KT - 1

    with ExitStack() as ctx:
        def sb(name, shape, dt=F32, stack=ctx):
            return stack.enter_context(nc.sbuf_tensor(name, shape, dt))

        def sem(name):
            return ctx.enter_context(nc.semaphore(name))

        ident = sb("ident", [P, P])
        cst = sb("cst", [P, KT, NC])
        tmp = sb("tmp", [P, 3, N])
        cx = sb("cx", [P, PADB + N])
        stat = sb("stat", [P, 24])
        raw = sb("raw", [P, RING, KT, P])
        w_hi = sb("w_hi", [P, RING, KT, P], F32R)
        w_lo = sb("w_lo", [P, RING, KT, P], F32R)
        xT = sb("xT", [P, KT, N])
        early = ExitStack()
        sb("act_tiles_0_to_7", [P, 2 * KT * N], F32R, early)
        v = sb("v", [P, KT, N], F32, early)
        gate_a = sb("gate_a", [P, KT, N], F32, early)
        y_b = sb("y_b", [P, KT, N], F32, early)
        UW = PADA + N
        u = sb("u", [P, KT, UW], F32, early)
        early.close()
        act = sb("act", [P, 2 * FT, N], F32R)
        FREE = KT * (3 * N + UW) - 2 * (FT - KT) * N
        sb("end_of_u", [P, FREE])
        middle = ExitStack()
        mid = sb("mid", [P, 2 * KT, N], F32R, middle)
        middle.close()
        final = ExitStack()
        y = sb("y", [P, TT + 1, D], F32, final)
        gf_row = sb("gf_row", [P, D], F32, final)
        sq_junk = sb("sq_junk", [P, D], F32, final)
        final.close()
        prods = sb("prods", [P, POOL_N - 1, SEQ])
        sb("mid_before_rows", [P, (TT + 3) * D - (POOL_N - 1) * SEQ])
        a_pack = sb("a_pack", [P, (PADA + B) * KT])
        tail_b = sb("tail_b", [P, PADB + B, KT])
        stage = sb("stage", [P, 4, P])
        assert (TT + 3) * D + (PADA + PADB + 2 * B) * KT + 4 * P <= 2 * KT * N and (TT + 3) * D >= (2 * KT - 3) * N

        psum = ctx.enter_context(nc.psum_tensor("psum", [P, 8, 512], F32))

        uf = u[:, :, :].rearrange("p t n -> p (t n)")
        tf = tmp[:, :, :].rearrange("p t n -> p (t n)")
        vf = v[:, :, :].rearrange("p t n -> p (t n)")
        gaf = gate_a[:, :, :].rearrange("p t n -> p (t n)")
        ybf = y_b[:, :, :].rearrange("p t n -> p (t n)")
        x_tok = [vf[:, t * D:(t + 1) * D] for t in range(TT)] + [ybf[0:B, D:2 * D]]
        TOK = [(TT, B)] + [(t, P) for t in range(TT)]
        Y_TOK = [(t, P) for t in range(TT - 1)] + [(TT, B)]
        crow = ybf[0:NC, 0:D]
        rms_inv = gate_a[:, 0, :]
        unit_row = gaf[:, N:N + P]
        diag = [gaf[:, N + (t + 1) * P:N + (t + 2) * P] for t in range(TT + 1)]
        u0 = KT * UW - FREE
        frow = uf[0:NCF, 0:FF]
        rinv = uf[:, u0:u0 + N]
        up_n = uf[:, u0 + N:u0 + 2 * N]
        cst_f = uf[:, u0 + 2 * N:u0 + 2 * N + FT * NCF].rearrange("p (t c) -> p t c", c=NCF)
        s2_at = u0 + 2 * N + FT * NCF
        ssum = uf[:, s2_at:s2_at + N]
        ones = uf[:, s2_at + N:s2_at + N + P]
        y_sq = ssum[:, 0:(TT + 1) * KT].rearrange("p (t n) -> p t n", n=KT)
        assert s2_at + N + P <= KT * UW and FF <= u0 + 2 * N
        tail_f = cst[:, :, :].rearrange("p t c -> p (t c)")[:, 0:(PADB + B) * FT].rearrange("p (r t) -> p r t", t=FT)
        t0, t1, t2 = (tmp[:, k, :] for k in range(3))
        h_tmp = [t0, t1, t2, cx[:, PADB:PADB + N]]
        win = t0[:, 0:B * WA].rearrange("p (b k) -> p b k", k=WA)
        win_w = t1[:, 0:B * WA].rearrange("p (b k) -> p b k", k=WA)
        SH = B * PADA // 2
        assert SH == PADA * KT // 2
        st_row = [ap.rearrange("p (h c) -> p h c", h=2) for ap in
                  (t1[0:SH, B * WA:B * WA + 2 * P], cx[0:SH, PADB:PADB + 2 * P])]
        f_stage = [t2[:, j * P:(j + 1) * P] for j in range(3)]
        vsum = cx[:, 0:N]
        ms, rs = stat[:, 0:5], stat[:, 5:10]
        win_sum = stat[:, 10:18]

        x_in = [sem(f"x_in{t}") for t in range(TT + 1)]
        rows_in, frows_in, gf_in, state_in = sem("rows_in"), sem("frows_in"), sem("gf_in"), [sem("state_in0"), sem("state_in1")]
        raw_in = [sem(f"raw_in{s}") for s in range(RING)]
        const_set, stat_set, ident_set = sem("const_set"), sem("stat_set"), sem("ident_set")
        cst_turned, cst_done = sem("cst_turned"), sem("cst_done")
        unit_set, x_squared, x_mean, x_root, x_inv, diag_done, rms_spread, rms_copied = (
            sem(n) for n in ("unit_set", "x_squared", "x_mean", "x_root", "x_inv", "diag_done", "rms_spread", "rms_copied"))
        x_turned, xT_done, hg_done, h_hi, h_lo_even, h_lo_odd = (
            sem(n) for n in ("x_turned", "xT_done", "hg_done", "h_hi", "h_lo_even", "h_lo_odd"))
        xT_half = sem("xT_half")
        hi_done, lo_done, mm_done, evicted = sem("hi_done"), sem("lo_done"), sem("mm_done"), sem("evicted")
        act_hi, act_lo, prod_done = sem("act_hi"), sem("act_lo"), sem("prod_done")
        u_done, prod_in, pool_sum, conv_b, tail_b_done = (sem(n) for n in ("u_done", "prod_in", "pool_sum", "conv_b", "tail_b_done"))
        tap_merged = sem("tap_merged")
        dve_tap = [sem(f"dve_tap{group}") for group in range(len(DVE_TAPS))]
        a_packed, a_turned, a_staged, state_turned, win_done, win_conv, v_done = (
            sem(n) for n in ("a_packed", "a_turned", "a_staged", "state_turned", "win_done", "win_conv", "v_done"))
        sum_zero, vsum_done, mean_done, frow_turned, cst_f_done = (
            sem(n) for n in ("sum_zero", "vsum_done", "mean_done", "frow_turned", "cst_f_done"))
        centred, squared, ssum_done, var_done, var_eps, var_root, rinv_done = (
            sem(n) for n in ("centred", "squared", "ssum_done", "var_done", "var_eps", "var_root", "rinv_done"))
        yb_gated, v_norm, v_sig, v_affine, table_set = (sem(n) for n in ("yb_gated", "v_norm", "v_sig", "v_affine", "table_set"))
        conv_f, fg_tail, silu_done = sem("conv_f"), sem("fg_tail"), sem("silu_done")
        f_turned, f_staged = sem("f_turned"), sem("f_staged")
        y_turned, y_scaled, y_squared, y_sq_set, y_sum, y_stat, y_root, y_inv, y_done = (
            sem(n) for n in ("y_turned", "y_scaled", "y_squared", "y_sq_set", "y_sum", "y_stat", "y_root", "y_inv", "y_done"))
        y_done_sc = sem("y_done_sc")
        old_out, state_out = sem("old_out"), sem("state_out")
        y_out = sem("y_out")

        def out_of(t):
            return t + 3

        def merged(i):
            return i + 3

        def summed(i, k):
            return (POOL_N - 1) * i + k + POOL_N

        def halves(ap):
            return ap.rearrange("p (a b) -> p a b", a=2)

        def tile(t, i, lo=0, hi=None):
            hi = t.shape[2] if hi is None else hi
            return t[:, bass.ds(i, 1), lo:hi].rearrange("p o n -> p (o n)")

        def scal(t, i, c):
            return t[:, bass.ds(i, 1), c:c + 1].rearrange("p o c -> p (o c)")

        def acc(s):
            return psum[:, 2 * (s % 2):2 * (s % 2) + 2, 0:H]

        stat_banks = psum[:, 6:8, 0:H]

        def kview(w, rows=None):
            w = w[0] if rows is None else w[0, rows[0]:rows[1], :]
            return w.rearrange("(k p) n -> p k n", p=P)

        wi = kview(w_in)
        COL = {"a_val": 0, "a_gate": D, "b_B": 2 * D, "b_C": 3 * D, "b_x": 4 * D, "g_A": 5 * D, "g_B": 6 * D}

        block = ctx.enter_context(nc.Block())

        @block.sync
        def _(sp):
            sp.dma_start(x_tok[TT], x_sample.rearrange("b s d -> (b s) d")).then_inc(x_in[TT], 16)
            for t in range(TT):
                if t == TT - 1:
                    for r, n, src in ((C_WA, WA, conv_a_w[0]), (C_BA, 1, conv_a_b), (C_LG, 1, ln_a_g), (C_LB, 1, ln_a_b),
                                      (C_GM, 1, g_mix), (C_GF, 1, g_ffn), (C_WB, WB, conv_b_w[0]),
                                      (C_SB, B * PADB, state_b[0].rearrange("b k c -> (b k) c"))):
                        sp.dma_start(crow[r:r + n, :], src).then_inc(rows_in, 16)
                sp.dma_start(x_tok[t], x_prompt[0, t * P:(t + 1) * P, :]).then_inc(x_in[t], 16)

            def load(g, s, src, k=KT):
                sp.wait_ge(lo_done, g - (RING - 1))
                sp.dma_start(raw[:, s, 0:k, :], src).then_inc(raw_in[s], 16)

            def pairs(first, names, w, it):
                for s in range(4):
                    c = names[s % 2] + (s // 2) * P + 2 * P * it
                    load(first + s, s, w[:, :, bass.ds(c, P)])

            for s in range(RING):
                c = (COL["a_val"], COL["a_gate"])[s % 2] + (s // 2) * P
                sp.dma_start(raw[:, s, :, :], wi[:, :, c:c + P]).then_inc(raw_in[s], 16)
            pairs(G_MIX + 4, (COL["b_C"], COL["b_x"]), wi, 0)
            with sp.Fori(1, KT // 2) as it:
                pairs(G_MIX + 8 * it, (COL["a_val"], COL["a_gate"]), wi, it)
                pairs(G_MIX + 8 * it + 4, (COL["b_C"], COL["b_x"]), wi, it)

            def plain(first, w, col):
                with sp.Fori(0, KT // RING) as it:
                    for s in range(RING):
                        load(first + RING * it + s, s, w[:, :, bass.ds(col + s * P + RING * P * it, P)])

            for old, new in ((state_a, a_sample), (state_b, b_sample), (state_f, f_sample)):
                k = old.shape[2]
                sp.dma_start(new[0, :, 0:k - 1, :], old[0, :, 1:k, :]).then_inc(old_out, 16)
            plain(G_B, wi, COL["b_B"])
            plain(G_BOUT, kview(w_b_out), 0)
            with sp.Fori(0, KT // 2) as it:
                pairs(G_GATE + 4 * it, (COL["g_A"], COL["g_B"]), wi, it)
            plain(G_AOUT, kview(w_a_out), 0)
            plain(G_O, kview(w_o), 0)
            wu = kview(w_up)
            with sp.Fori(0, FT // 2) as it:
                pairs(G_UP + 4 * it, (0, FF), wu, it)
            wd = kview(w_down)
            with sp.Fori(0, KT) as n:
                for s in range(RING):
                    load(G_DOWN + RING * n + s, s,
                         wd[:, KFIRST[s]:KFIRST[s] + KSPLIT[s], bass.ds(P * n, P)], KSPLIT[s])

            for j, (t, n) in enumerate(Y_TOK):
                sp.wait_ge(y_done, j + 1)
                out = y_prompt[0, t * P:(t + 1) * P, :] if t < TT else y_sample.rearrange("b s d -> (b s) d")
                sp.dma_start(out, y[0:n, t, :]).then_inc(y_out, 16)
            sp.wait_ge(y_out, 16 * (TT + 1))
            sp.wait_ge(old_out, 16 * 3)
            sp.wait_ge(state_out, 16 * 8)

        @block.gpsimd
        def _(pool):
            pool.sem_inc(pool_sum, summed(0, 0))
            pool.memset(ident[:, :], 0.0).then_inc(ident_set, 1)
            pool.wait_ge(ident_set, 1)
            pool.affine_select(out=ident[:, :], in_=ident[:, :], compare_op=ALU.not_equal, fill=1.0, base=0,
                               pattern=[[-1, P]], channel_multiplier=1).then_inc(ident_set, 1)
            pool.memset(u[:, :, 0:PADA], 0.0).then_inc(const_set, 1)
            pool.memset(cx[:, 0:PADB], 0.0).then_inc(const_set, 1)
            pool.wait_ge(const_set, 2)
            for k in range(1, KT, 2):
                pool.wait_ge(h_hi, k + 1)
                pool.tensor_tensor(act[:, 2 * k + 1, :], h_tmp[k % 4], act[:, 2 * k, :], ALU.subtract).then_inc(h_lo_odd, 1)
            for i in range(KT):
                part = gate_a[:, i, 0:SEQ]
                for k in range(1, POOL_N):
                    pool.wait_ge(prod_in, POOL_N * i + k + 1)
                    pool.wait_ge(pool_sum, summed(i, k - 1))
                    pool.tensor_tensor(part, part, prods[:, k - 1, :], ALU.add).then_inc(pool_sum, 1)

        @block.scalar
        def _(sc):
            for started in (tail_b_done, win_done, fg_tail, silu_done, y_squared):
                sc.sem_inc(started, START)

            def hi_split(g, s, k=KT, first=False):
                if first:
                    sc.wait_ge(raw_in[s], 16)
                else:
                    sc.wait_ge(raw_in[s], (g - s) * (16 // RING) + 16)
                    sc.wait_ge(mm_done, g - (RING - 1))
                sc.activation(w_hi[:, s, 0:k, :], raw[:, s, 0:k, :], ACT.Copy).then_inc(hi_done, 1)

            def evict(g, s, out, func):
                sc.wait_ge(mm_done, g + 1)
                sc.wait_ge(evicted, out_of(g - 1))
                sc.activation(halves(out), acc(s), func).then_inc(evicted, 1)

            def act_hi_split(out, src, sem_, value, scale=None):
                sc.wait_ge(sem_, value)
                if scale is None:
                    sc.activation(out, src, ACT.Copy).then_inc(act_hi, 1)
                else:
                    sc.activation(out, src, ACT.Copy, scale=scale).then_inc(act_hi, 1)

            sc.wait_ge(stat_set, 1)
            sc.activation(rs, ms, ACT.Sqrt).then_inc(table_set, 1)
            for j, (t, n) in enumerate(TOK):
                sc.wait_ge(x_in[t], 16)
                if j > 0:
                    sc.wait_ge(x_squared, j)
                sc.activation(tf[0:n, 0:D], x_tok[t], ACT.Square, accum_out=stat[0:n, 18 + t:19 + t]).then_inc(x_squared, 1)
                sc.wait_ge(x_mean, j + 1)
                sc.activation(rs[0:n, t:t + 1], ms[0:n, t:t + 1], ACT.Sqrt).then_inc(x_root, 1)
            sc.wait_ge(cst_turned, 1)
            sc.activation(cst[:, :, :], psum[:, 6, 0:KT * NC].rearrange("p (t c) -> p t c", c=NC), ACT.Copy).then_inc(cst_done, 1)
            sc.activation(rms_inv[:, SEQ:N], psum[:, 6, KT * NC:KT * NC + B], ACT.Copy).then_inc(rms_copied, 1)
            sc.wait_ge(x_turned, TT + 1)
            sc.activation(xT[:, 0:KT // 2, SEQ - P:SEQ], psum[:, 2 * (TT % 3), :].rearrange("p (k n) -> p k n", k=4),
                          ACT.Copy).then_inc(xT_half, 1)
            sc.wait_ge(rms_spread, TT + 1)
            sc.activation(rms_inv[:, 0:SEQ], psum[:, 7, 0:SEQ], ACT.Copy).then_inc(rms_copied, 1)
            hi_split(0, 0, first=True)
            for k in range(KT):
                if k == 2:
                    hi_split(1, 1, first=True)
                sc.wait_ge(hg_done, k + 1)
                sc.activation(act[:, 2 * k, :], h_tmp[k % 4], ACT.Copy).then_inc(h_hi, 1)
            for s in range(2, RING):
                hi_split(s, s, first=True)
            sc.activation(rs, ms, ACT.Sigmoid).then_inc(table_set, 1)

            def products(i, first, last):
                for k in range(first, last):
                    if k == 0:
                        sc.wait_ge(u_done, START + i + 1)
                        out = tile(gate_a, i, 0, SEQ)
                    else:
                        sc.wait_ge(pool_sum, summed(i - 1, k))
                        out = prods[:, k - 1, :]
                    sc.activation(out, tile(u, i, k, k + SEQ), ACT.Copy, scale=scal(cst, i, C_WA + k)).then_inc(prod_in, 1)

            prod_cuts = {2: ((0, 0, 4),), 3: ((0, 4, 8),), 4: ((0, 8, POOL_N), (1, 0, 1)), 5: ((1, 1, 4),), 6: ((1, 4, 8),),
                         7: ((1, 8, POOL_N),)}
            with sc.Fori(0, KT // 2) as it:
                for s in range(8):
                    g = G_MIX + 8 * it + s
                    i = 2 * it + (s % 4) // 2
                    if s in (0, 2, 1, 3):
                        sc.wait_ge(u_done, START + i)
                        evict(g, s, t0 if s % 2 == 0 else t1, ACT.Copy if s % 2 == 0 else ACT.Sigmoid)
                    elif s % 2 == 0:
                        sc.wait_ge(u_done, START + 2 * it + 2)
                        evict(g, s, t0, ACT.Copy)
                    hi_split(g + RING, s % RING)
                    for odd, a, b in prod_cuts.get(s, ()):
                        products(2 * it + odd, a, b)
                    if s in (5, 7):
                        sc.wait_ge(evicted, out_of(g))
                        sc.activation(tail_b[:, :, bass.ds(i, 1)].rearrange("p r o -> p (r o)"), cx[:, SEQ:SEQ + PADB + B],
                                      ACT.Copy).then_inc(tail_b_done, 1)

            def load_state(i):
                src = state_a[0].rearrange("b k c -> (b k) c")[:, i * P:(i + 1) * P]
                sc.dma_start(st_row[i % 2], src.rearrange("(h p) c -> p h c", h=2)).then_inc(state_in[i % 2], 16)

            sc.wait_ge(u_done, START + KT)
            load_state(0)
            for c, n, first in ((0, PADA, SEQ), (PADA * KT, B, PADA + SEQ)):
                sc.activation(a_pack[:, c:c + n * KT].rearrange("p (r t) -> p t r", t=KT), u[:, :, first:first + n],
                              ACT.Copy).then_inc(a_packed, 1)
            def state_tile(i):
                sc.wait_ge(state_turned, i + 1)
                if i + 2 < KT:
                    load_state(i + 2)
                if i > 0:
                    sc.wait_ge(win_conv, START + 3 * i)
                sc.activation(win[:, :, 0:PADA], psum[:, 4, 0:B * PADA].rearrange("p (b k) -> p b k", k=PADA),
                              ACT.Copy).then_inc(win_done, 1)
                sc.activation(win[:, :, PADA:WA].rearrange("p b k -> p (b k)"), tile(u, i, PADA + SEQ, UW),
                              ACT.Copy).then_inc(win_done, 1)

            def b_step(i, s):
                state_tile(i)
                sc.wait_ge(pool_sum, summed(KT - 1, POOL_N - 1))
                act_hi_split(tile(mid, 2 * i), t2, evicted, out_of(G_B + i))
                hi_split(G_B + RING + i, s)

            sc.wait_ge(conv_b, START + 6 * KT)
            load_state(1)
            for s in range(RING):
                b_step(s, s)
            nb = PADB * KT
            sc.wait_ge(a_turned, 4)
            for j, n in enumerate((SH, SH, B * KT, nb + B * KT)):
                sc.activation(stage[0:n, j, :], psum[0:n, 5, j * P:(j + 1) * P], ACT.Copy).then_inc(a_staged, 1)
            rows = lambda ap: ap.rearrange("r (t c) -> (r t) c", c=P)
            last_rows = lambda ap, k: ap[0, :, k - 1, :].rearrange("b (t c) -> b t c", c=P)
            for j, out, src in ((0, rows(a_prompt[0, 0])[0:SH, :], stage[0:SH, 0, :]),
                                (1, rows(a_prompt[0, 0])[SH:2 * SH, :], stage[0:SH, 1, :]),
                                (2, last_rows(a_sample, PADA), stage[0:B * KT, 2, :]),
                                (3, rows(b_prompt[0, 0]), stage[0:nb, 3, :]),
                                (3, last_rows(b_sample, PADB), stage[nb:nb + B * KT, 3, :])):
                sc.wait_ge(a_staged, j + 1)
                sc.dma_start(out, src).then_inc(state_out, 16)
            for s in range(RING):
                if s == 2:
                    sc.wait_ge(state_out, 16 * 5)
                b_step(RING + s, s)

            with sc.Fori(0, KT // RING) as it:
                for s in range(RING):
                    i = RING * it + s
                    evict(G_BOUT + i, s, tile(y_b, i), ACT.Copy)
                    hi_split(G_BOUT + RING + i, s)
            def gate_step(it, s):
                g = G_GATE + RING * it + s
                i = 2 * it + s // 2
                if s % 2 == 0:
                    evict(g, s, tile(gate_a, i), ACT.Sigmoid)
                else:
                    sc.wait_ge(yb_gated, START + i)
                    evict(g, s, t1, ACT.Sigmoid)
                hi_split(g + RING, s)

            def square(t):
                sc.wait_ge(centred, t + 1)
                if t > 0:
                    sc.wait_ge(ssum_done, START + t)
                sc.activation(t0, v[:, t, :], ACT.Square).then_inc(squared, 1)

            def swish(t):
                sc.wait_ge(v_norm, t + 1)
                sc.wait_ge(prod_done, START + t)
                sc.activation(t0, v[:, t, :], ACT.Sigmoid, scale=cst[:, t, C_LG:C_LG + 1],
                              bias=cst[:, t, C_LB:C_LB + 1]).then_inc(v_sig, 1)
                sc.activation(v[:, t, :], v[:, t, :], ACT.Identity, scale=cst[:, t, C_LG:C_LG + 1],
                              bias=cst[:, t, C_LB:C_LB + 1]).then_inc(v_affine, 1)

            for step in range(2 * KT):
                if step == 2:
                    sc.wait_ge(v_done, KT)
                    sc.wait_ge(win_done, START + 2 * KT)
                    sc.dma_start(frow[0:CF_W, :], state_f[0].rearrange("b k c -> (b k) c")).then_inc(frows_in, 16)
                    sc.dma_start(frow[CF_W:NCF, :], conv_f_w[0]).then_inc(frows_in, 16)
                if step in SQUARE_STEPS:
                    for t in SQUARE_STEPS[step]:
                        square(t)
                if step == ROOT_STEP - 1:
                    sc.wait_ge(frow_turned, 1)
                    sc.activation(cst_f, psum[:, 4, 0:FT * NCF].rearrange("p (t c) -> p t c", c=NCF), ACT.Copy).then_inc(cst_f_done, 1)
                if step == ROOT_STEP:
                    sc.wait_ge(var_eps, 1)
                    sc.activation(rinv, rinv, ACT.Sqrt).then_inc(var_root, 1)
                    sc.activation(rs, ms, ACT.Sigmoid).then_inc(table_set, 1)
                if step >= KT:
                    t = step - KT
                    act_hi_split(mid[:, 2 * t, :], t2, prod_done, START + t + 1)
                    if t + 1 < KT:
                        swish(t + 1)
                gate_step(step // RING, step % RING)
                if step == ROOT_STEP:
                    swish(0)

            with sc.Fori(0, KT // RING) as it:
                for s in range(RING):
                    i = RING * it + s
                    act_hi_split(tile(act, 2 * i), t2, prod_done, START + KT + i + 1)
                    hi_split(G_AOUT + RING + i, s)

            with sc.Fori(0, KT // RING) as it:
                for s in range(RING):
                    i = RING * it + s
                    sc.wait_ge(ssum_done, START + KT + i)
                    act_hi_split(tile(mid, 2 * i), tile(xT, i), evicted, out_of(G_O + i), scal(cst, i, C_GF))
                    sc.activation(t0, tile(xT, i), ACT.Square).then_inc(squared, 1)
                    hi_split(G_O + RING + i, s)
            sc.wait_ge(var_eps, 2)
            sc.activation(rinv, rinv, ACT.Sqrt).then_inc(var_root, 1)
            sc.activation(rs, ms, ACT.Silu).then_inc(table_set, 1)

            with sc.Fori(0, FT // 2) as it:
                for s in range(RING):
                    g = G_UP + RING * it + s
                    i = 2 * it + s // 2
                    hi_split(g + RING, s)
                    if s % 2 == 0:
                        sc.wait_ge(evicted, out_of(g))
                        sc.activation(tail_f[:, :, bass.ds(i, 1)].rearrange("p r o -> p (r o)"),
                                      cx[:, SEQ:SEQ + PADB + B], ACT.Copy).then_inc(fg_tail, 1)
                        sc.wait_ge(conv_f, START + 6 * i + 6)
                        sc.wait_ge(prod_done, START + 2 * KT + i)
                        sc.activation(t1, t0, ACT.Silu).then_inc(silu_done, 1)
                    else:
                        act_hi_split(tile(act, 2 * i), t2, prod_done, START + 2 * KT + i + 1)

            sc.wait_ge(mm_done, G_DOWN)
            sc.dma_start(gf_row[:, :], g_final.rearrange("(o d) -> o d", o=1).broadcast_to([P, D])).then_inc(gf_in, 16)
            nf, hb = PADB * FT, B // 2
            sc.wait_ge(act_lo, START + S_G + FT)
            for j in range(3):
                sc.wait_ge(f_turned, j + 1)
                n = nf if j == 0 else hb * FT
                sc.activation(f_stage[j][0:n, :], psum[0:n, 4 + j, 0:P], ACT.Copy).then_inc(f_staged, 1)
                sc.wait_ge(f_staged, j + 1)
                if j == 0:
                    sc.dma_start(f_prompt[0, 0].rearrange("r (t c) -> (r t) c", c=P), f_stage[j][0:n, :]).then_inc(state_out, 16)
                else:
                    sc.dma_start(f_sample[0, (j - 1) * hb:j * hb, PADB - 1, :].rearrange("b (t c) -> b t c", c=P),
                                 f_stage[j][0:n, :]).then_inc(state_out, 16)
            sc.activation(rs, ms, ACT.Sqrt).then_inc(table_set, 1)

            def y_square(n, par):
                for t in range(TT + 1):
                    rows = P if t < TT else B
                    src = psum[:, 4 + 2 * par, t * P:(t + 1) * P] if t < TT else psum[0:B, 5 + 2 * par, 0:P]
                    sc.activation(sq_junk[0:rows, t * P:(t + 1) * P], src, ACT.Square,
                                  accum_out=y_sq[0:rows, t, bass.ds(n, 1)]).then_inc(y_squared, 1)

            def down_split(n, s):
                hi_split(G_DOWN + RING * n + RING + s, s, KSPLIT[s])

            sc.wait_ge(y_sq_set, 1)
            for s in range(RING):
                down_split(0, s)
            with sc.Fori(0, KT // 2 - 1) as it:
                for par in range(2):
                    n = 2 * it + par
                    down_split(n + 1, 0)
                    sc.wait_ge(y_scaled, START + 2 * n + 2)
                    sc.wait_ge(y_squared, START + (TT + 1) * n)
                    down_split(n + 1, 1)
                    y_square(n, par)
                    down_split(n + 1, 2)
                    down_split(n + 1, 3)
            for n in (KT - 2, KT - 1):
                sc.wait_ge(y_scaled, START + 2 * n + 2)
                sc.wait_ge(y_squared, START + (TT + 1) * n)
                y_square(n, n % 2)
            sc.wait_ge(y_stat, 1)
            sc.activation(rs, ms, ACT.Sqrt).then_inc(y_root, 1)
            sc.wait_ge(y_inv, 1)
            sc.activation(y[:, TT - 1, :], y[:, TT - 1, :], ACT.Copy, scale=rs[:, TT - 1:TT]).then_inc(y_done_sc, 1)
            sc.wait_ge(y_done_sc, 1)
            sc.dma_start(y_prompt[0, SEQ - P:SEQ, :], y[:, TT - 1, :]).then_inc(y_out, 16)

        @block.vector
        def _(ve):
            for started in (y_scaled, u_done, conv_b, win_conv, vsum_done, ssum_done, yb_gated, prod_done, conv_f, act_lo):
                ve.sem_inc(started, START)
            ve.sem_inc(evicted, out_of(-1))
            ve.sem_inc(tap_merged, merged(-1))
            ve.memset(stat[:, :], 1.0).then_inc(stat_set, 1)

            def lo_split(g, s, k=KT, first=False):
                ve.wait_ge(hi_done, g + 1)
                if not first:
                    ve.wait_ge(mm_done, g - (RING - 1))
                ve.tensor_tensor(w_lo[:, s, 0:k, :], raw[:, s, 0:k, :], w_hi[:, s, 0:k, :], ALU.subtract).then_inc(lo_done, 1)

            def act_lo_split(out, src, hi, a):
                ve.wait_ge(act_hi, a + 1)
                ve.tensor_tensor(out, src, hi, ALU.subtract).then_inc(act_lo, 1)

            def out_of_psum(g, t):
                ve.wait_ge(mm_done, g + 1)
                ve.wait_ge(evicted, out_of(t - 1))

            def copy_xT(j):
                t, n = TOK[j]
                ve.wait_ge(x_turned, j + 1)
                pair = 2 * (j % 3)
                ve.tensor_scalar(xT[:, :, t * P:t * P + n].rearrange("p (b k) n -> p b k n", b=2),
                                 psum[:, pair:pair + 2, :].rearrange("p b (k n) -> p b k n", k=4)[:, :, :, 0:n],
                                 1.0, None, ALU.mult).then_inc(xT_done, 1)

            ve.memset(unit_row, 1.0).then_inc(unit_set, 1)
            ve.wait_ge(ident_set, 2)
            for j, (t, n) in enumerate(TOK):
                ve.wait_ge(x_squared, j + 1)
                ve.tensor_scalar(ms[0:n, t:t + 1], stat[0:n, 18 + t:19 + t], 1.0 / D, RMS_EPS, ALU.mult, ALU.add).then_inc(x_mean, 1)
                if 0 < j < TT:
                    copy_xT(j - 1)
                ve.wait_ge(x_root, j + 1)
                ve.reciprocal(rs[0:n, t:t + 1], rs[0:n, t:t + 1]).then_inc(x_inv, 1)
                ve.wait_ge(x_inv, j + 1)
                ve.tensor_scalar(diag[t][0:n, 0:n], ident[0:n, 0:n], rs[0:n, t:t + 1], None, ALU.mult).then_inc(diag_done, 1)
            copy_xT(TT - 1)
            ve.wait_ge(x_turned, TT + 1)
            ve.tensor_scalar(xT[:, KT // 2:KT, SEQ - P:SEQ], psum[:, 2 * (TT % 3) + 1, :].rearrange("p (k n) -> p k n", k=4),
                             1.0, None, ALU.mult).then_inc(xT_done, 1)
            ve.wait_ge(xT_done, TT + 1)
            ve.wait_ge(xT_half, 1)
            ve.wait_ge(cst_done, 1)
            ve.wait_ge(rms_copied, 2)
            ve.wait_ge(const_set, 2)
            for k in range(KT):
                if k >= 4:
                    ve.wait_ge((h_lo_even, h_lo_odd)[k % 2], k // 2 - 1)
                ve.scalar_tensor_tensor(out=h_tmp[k % 4], in0=xT[:, k, :], scalar=cst[:, k, C_GM:C_GM + 1], in1=rms_inv,
                                        op0=ALU.mult, op1=ALU.mult).then_inc(hg_done, 1)
                if k % 2 == 1:
                    ve.wait_ge(h_hi, k)
                    ve.tensor_tensor(act[:, 2 * k - 1, :], h_tmp[(k - 1) % 4], act[:, 2 * k - 2, :],
                                     ALU.subtract).then_inc(h_lo_even, 1)
            for s in range(RING):
                lo_split(s, s, first=True)

            def mix_taps(i, par, first, last):
                for k in range(first, last):
                    src, w = tile(u, i, POOL_N + k, POOL_N + k + SEQ), scal(cst, i, C_WA + POOL_N + k)
                    out = psum[:, 4 + 2 * par + k % 2, 0:SEQ]
                    if k == 0:
                        ve.wait_ge(u_done, START + i + 1)
                        ve.wait_ge(tap_merged, merged(i - 2))
                        ve.tensor_scalar(out, src, w, scal(cst, i, C_BA), ALU.mult, ALU.add).then_inc(dve_tap[0], 1)
                    elif k == 1:
                        ve.tensor_scalar(out, src, w, None, ALU.mult).then_inc(dve_tap[0], 1)
                    else:
                        ve.wait_ge(dve_tap[0], MIX_N * i + k - 1)
                        ve.scalar_tensor_tensor(out=tile(v, i, 0, SEQ) if k == MIX_N - 2 else out, in0=src, scalar=w,
                                                in1=out, op0=ALU.mult, op1=ALU.add).then_inc(dve_tap[0], 1)
                if last == MIX_N:
                    ve.wait_ge(dve_tap[0], MIX_N * i + MIX_N)
                    ve.tensor_tensor(tile(v, i, 0, SEQ), psum[:, 4 + 2 * par + (MIX_N - 1) % 2, 0:SEQ], tile(v, i, 0, SEQ),
                                     ALU.add).then_inc(tap_merged, 1)

            def taps(i, group, first, last):
                for j in range(first, last):
                    k = TAP_CUTS[group] + j
                    for half, (lo, hi) in enumerate(((0, SEQ // 2), (SEQ // 2, SEQ))):
                        src, w = tile(u, i, POOL_N + k + lo, POOL_N + k + hi), scal(cst, i, C_WA + POOL_N + k)
                        out = tile(v, i, lo, hi)
                        if j > 0:
                            ve.wait_ge(dve_tap[group], 2 * (DVE_TAPS[group] * i + j) + half - 1)
                        elif group == 1:
                            ve.wait_ge(tap_merged, merged(i))
                        else:
                            ve.wait_ge(dve_tap[group - 1], 2 * DVE_TAPS[group - 1] * (i + 1))
                        ve.scalar_tensor_tensor(out=out, in0=src, scalar=w, in1=out, op0=ALU.mult,
                                                op1=ALU.add).then_inc(dve_tap[group], 1)

            def narrow(i, out_main, out_side, w, w_c, state, s_c, done):
                for k in range(WB):
                    wk = scal(w, i, w_c + k)
                    side = cx[:, PADB + SEQ:PADB + N] if k == PADB else \
                        state[:, bass.ds(i, 1), s_c + k:s_c + B * PADB:PADB].rearrange("p o b -> p (o b)")
                    for j, (out, src) in enumerate(((out_main, cx[:, k:k + SEQ]), (out_side, side))):
                        if k == 0:
                            ve.tensor_scalar(out, src, wk, None, ALU.mult).then_inc(done, 1)
                        else:
                            ve.wait_ge(done, START + 6 * i + 2 * k + j - 1)
                            ve.scalar_tensor_tensor(out=out, in0=src, scalar=wk, in1=out, op0=ALU.mult,
                                                    op1=ALU.add).then_inc(done, 1)

            cuts = {0: ((-1, 10, MIX_N),), 1: ((0, 0, 4),), 2: ((0, 4, 9),), 3: ((0, 9, 13),), 4: ((0, 13, MIX_N), (1, 0, 3)),
                    5: ((1, 3, 4),), 6: ((1, 4, 9),), 7: ((1, 9, 10),)}

            def mix_steps(it, first=False):
                for s in range(8):
                    g = G_MIX + 8 * it + s
                    i = 2 * it + (s % 4) // 2
                    if s in (1, 3):
                        ve.wait_ge(evicted, out_of(g))
                        ve.tensor_tensor(tile(u, i, PADA, UW), t0, t1, ALU.mult).then_inc(u_done, 1)
                    if s in (5, 7):
                        out_of_psum(g, g)
                        ve.wait_ge(tail_b_done, START + i)
                        ve.wait_ge(conv_b, START + 6 * i)
                        ve.tensor_tensor(halves(cx[:, PADB:PADB + N]), acc(s), halves(t0), ALU.mult).then_inc(evicted, 1)
                    lo_split(g + RING, s % RING)
                    if s in (5, 7):
                        ve.wait_ge(evicted, out_of(g))
                        narrow(i, tile(y_b, i, 0, SEQ), tile(y_b, i, SEQ, N), cst, C_WB, cst, C_SB, conv_b)
                    for tile_less, a, b in cuts[s]:
                        if not (first and tile_less < 0):
                            mix_taps(2 * it + tile_less, tile_less % 2, a, b)

            mix_steps(0, first=True)
            with ve.Fori(1, KT // 2) as it:
                mix_steps(it)

            def b_step(i, s, left=None):
                out_of_psum(G_B + i, G_B + i)
                ve.wait_ge(act_lo, START + i)
                ve.wait_ge(conv_b, START + 6 * KT)
                ve.tensor_tensor(halves(t2), acc(s), halves(tile(y_b, i)), ALU.mult).then_inc(evicted, 1)
                taps(i, 1, 0, 1)
                act_lo_split(tile(mid, 2 * i + 1), t2, tile(mid, 2 * i), S_Q + i)
                lo_split(G_B + RING + i, s)
                ve.wait_ge(win_done, START + 2 * i + 2)
                wa = cst[:, bass.ds(i, 1), C_WA:C_WA + WA].broadcast_to([P, B, WA])
                ve.tensor_tensor(win_w, win, wa, ALU.mult).then_inc(win_conv, 1)
                ve.wait_ge(win_conv, START + 3 * i + 1)
                ve.tensor_reduce(win_sum, win_w, X, ALU.add).then_inc(win_conv, 1)
                taps(i, 1, 1, DVE_TAPS[1])
                ve.wait_ge(win_conv, START + 3 * i + 2)
                ve.tensor_scalar(tile(v, i, SEQ, N), win_sum, scal(cst, i, C_BA), None, ALU.add).then_inc(win_conv, 1)
                if left is not None:
                    mix_taps(KT - 1, 1, *left)

            for s, left in enumerate(((10, 12), (12, 13), (13, 14), (14, MIX_N))):
                b_step(s, s, left)
            with ve.Fori(1, KT // RING) as it:
                for s in range(RING):
                    b_step(RING * it + s, s)

            ve.wait_ge(tail_b_done, START + KT)
            ve.memset(vsum, 0.0).then_inc(sum_zero, 1)
            ve.wait_ge(sum_zero, 1)
            ve.wait_ge(win_conv, START + 3 * KT)
            with ve.Fori(0, KT // RING) as it:
                for s in range(RING):
                    i = RING * it + s
                    taps(i, 2, 0, DVE_TAPS[2])
                    lo_split(G_BOUT + RING + i, s)
                    ve.wait_ge(pool_sum, summed(i, POOL_N - 1))
                    ve.wait_ge(dve_tap[2], 2 * DVE_TAPS[2] * (i + 1))
                    ve.tensor_tensor(tile(v, i, 0, SEQ), tile(v, i, 0, SEQ), tile(gate_a, i, 0, SEQ), ALU.add).then_inc(v_done, 1)
                    ve.wait_ge(v_done, i + 1)
                    ve.wait_ge(vsum_done, START + i)
                    ve.tensor_tensor(vsum, vsum, tile(v, i), ALU.add).then_inc(vsum_done, 1)
            ve.memset(ones, 1.0 / D).then_inc(sum_zero, 1)
            ve.memset(ssum, 0.0).then_inc(sum_zero, 1)
            ve.wait_ge(sum_zero, 3)

            def gate_step(it, s):
                g = G_GATE + RING * it + s
                if s % 2 == 1:
                    i = 2 * it + s // 2
                    ve.wait_ge(evicted, out_of(g))
                    ve.tensor_tensor(tile(y_b, i), tile(y_b, i), t1, ALU.mult).then_inc(yb_gated, 1)
                lo_split(g + RING, s)

            def square_sum(t, at):
                ve.wait_ge(squared, at + t + 1)
                ve.wait_ge(ssum_done, START + at + t)
                ve.tensor_tensor(ssum, ssum, t0, ALU.add).then_inc(ssum_done, 1)

            def root(n, eps):
                ve.wait_ge(var_done, n)
                ve.tensor_scalar(halves(rinv), stat_banks, eps, None, ALU.add).then_inc(var_eps, 1)
                ve.wait_ge(var_root, n)
                ve.reciprocal(rinv, rinv).then_inc(rinv_done, 1)
                ve.wait_ge(rinv_done, n)

            for step in range(2 * KT):
                if step in SQUARE_STEPS:
                    if step == min(SQUARE_STEPS):
                        ve.wait_ge(mean_done, 1)
                    for t in SQUARE_STEPS[step]:
                        ve.tensor_tensor(halves(v[:, t, :]), halves(v[:, t, :]), stat_banks, ALU.subtract).then_inc(centred, 1)
                if step == ROOT_STEP:
                    ve.wait_ge(frow_turned, 1)
                    root(1, LN_EPS)
                    ve.memset(ssum, 0.0).then_inc(sum_zero, 1)
                    ve.tensor_tensor(v[:, 0, :], v[:, 0, :], rinv, ALU.mult).then_inc(v_norm, 1)
                if step >= KT:
                    t = step - KT
                    ve.wait_ge(v_affine, t + 1)
                    ve.wait_ge(act_lo, START + S_V + t)
                    ve.tensor_tensor(t2, v[:, t, :], t0, ALU.mult).then_inc(prod_done, 1)
                    if t + 1 < KT:
                        ve.tensor_tensor(v[:, t + 1, :], v[:, t + 1, :], rinv, ALU.mult).then_inc(v_norm, 1)
                    act_lo_split(mid[:, 2 * t + 1, :], t2, mid[:, 2 * t, :], S_V + t)
                if step in SQUARE_STEPS:
                    square_sum(SQUARE_STEPS[step][0], 0)
                gate_step(step // RING, step % RING)
                if step in SQUARE_STEPS:
                    square_sum(SQUARE_STEPS[step][1], 0)

            ve.wait_ge(yb_gated, START + KT)
            with ve.Fori(0, KT // RING) as it:
                for s in range(RING):
                    i = RING * it + s
                    g = G_AOUT + i
                    out_of_psum(g, g)
                    ve.wait_ge(prod_done, START + KT + i)
                    ve.tensor_tensor(halves(t1), acc(s), halves(tile(gate_a, i)), ALU.mult).then_inc(evicted, 1)
                    ve.wait_ge(evicted, out_of(g))
                    ve.wait_ge(act_lo, START + S_M + i)
                    ve.tensor_tensor(t2, t1, tile(y_b, i), ALU.add).then_inc(prod_done, 1)
                    act_lo_split(tile(act, 2 * i + 1), t2, tile(act, 2 * i), S_M + i)
                    lo_split(g + RING, s)

            ve.wait_ge(sum_zero, 4)
            with ve.Fori(0, KT // RING) as it:
                for s in range(RING):
                    i = RING * it + s
                    g = G_O + i
                    out_of_psum(g, g)
                    ve.tensor_tensor(halves(tile(xT, i)), acc(s), halves(tile(xT, i)), ALU.add).then_inc(evicted, 1)
                    ve.wait_ge(act_hi, S_H + i + 1)
                    ve.wait_ge(evicted, out_of(g))
                    ve.scalar_tensor_tensor(out=tile(mid, 2 * i + 1), in0=tile(xT, i), scalar=scal(cst, i, C_GF),
                                            in1=tile(mid, 2 * i), op0=ALU.mult, op1=ALU.subtract).then_inc(act_lo, 1)
                    square_sum(i, KT)
                    lo_split(g + RING, s)
            root(2, RMS_EPS)
            ve.memset(cx[:, 0:PADB], 0.0).then_inc(sum_zero, 1)
            ve.wait_ge(sum_zero, 5)
            ve.wait_ge(cst_f_done, 1)

            with ve.Fori(0, FT // 2) as it:
                for s in range(RING):
                    g = G_UP + RING * it + s
                    i = 2 * it + s // 2
                    out_of_psum(g, g)
                    if s % 2 == 0:
                        ve.wait_ge(fg_tail, START + i)
                        ve.wait_ge(conv_f, START + 6 * i)
                        ve.wait_ge(silu_done, START + i)
                        ve.tensor_tensor(halves(cx[:, PADB:PADB + N]), acc(s), halves(rinv), ALU.mult).then_inc(evicted, 1)
                        ve.wait_ge(evicted, out_of(g))
                        narrow(i, t0[:, 0:SEQ], t0[:, SEQ:N], cst_f, CF_W, cst_f, 0, conv_f)
                        lo_split(g + RING, s)
                    else:
                        ve.tensor_tensor(halves(up_n), acc(s), halves(rinv), ALU.mult).then_inc(evicted, 1)
                        ve.wait_ge(evicted, out_of(g))
                        ve.wait_ge(silu_done, START + i + 1)
                        ve.wait_ge(act_lo, START + S_G + i)
                        ve.tensor_tensor(t2, up_n, t1, ALU.mult).then_inc(prod_done, 1)
                        lo_split(g + RING, s)
                        act_lo_split(tile(act, 2 * i + 1), t2, tile(act, 2 * i), S_G + i)

            def down_split(n, s):
                lo_split(G_DOWN + RING * n + RING + s, s, KSPLIT[s])

            def down_out(n, par):
                ve.wait_ge(mm_done, G_DOWN + RING * n + RING)
                ve.wait_ge(evicted, out_of(G_DOWN + n - 1))
                ve.wait_ge(y_turned, START + n)
                ve.tensor_tensor(halves((t0, t1)[par]), acc(par), halves(tile(xT, n)), ALU.add).then_inc(evicted, 1)

            def y_scale(n, par):
                ve.wait_ge(y_turned, START + n + 1)
                at = bass.ds(P * n, P)
                ve.tensor_tensor(y[:, 0:TT, at], psum[:, 4 + 2 * par, :].rearrange("p (t c) -> p t c", c=P),
                                 gf_row[:, at].rearrange("p (o c) -> p o c", o=1).broadcast_to([P, TT, P]),
                                 ALU.mult).then_inc(y_scaled, 1)
                ve.tensor_tensor(y[0:B, TT, at], psum[0:B, 5 + 2 * par, 0:P], gf_row[0:B, at], ALU.mult).then_inc(y_scaled, 1)

            ve.memset(y_sq, 1.0).then_inc(y_sq_set, 1)
            for s in range(RING - 1):
                down_split(0, s)
            down_out(0, 0)
            down_split(0, RING - 1)
            ve.wait_ge(gf_in, 16)
            with ve.Fori(0, KT // 2 - 1) as it:
                for par in range(2):
                    n = 2 * it + par
                    down_split(n + 1, 0)
                    y_scale(n, par)
                    down_split(n + 1, 1)
                    down_split(n + 1, 2)
                    down_out(n + 1, 1 - par)
                    down_split(n + 1, 3)
            y_scale(KT - 2, 0)
            down_out(KT - 1, 1)
            y_scale(KT - 1, 1)
            ve.wait_ge(y_squared, START + (TT + 1) * KT)
            ve.tensor_reduce(stat[:, 18:18 + TT + 1], y_sq, X, ALU.add).then_inc(y_sum, 1)
            ve.wait_ge(y_sum, 1)
            ve.tensor_scalar(ms, stat[:, 18:18 + TT + 1], 1.0 / D, RMS_EPS, ALU.mult, ALU.add).then_inc(y_stat, 1)
            ve.wait_ge(y_root, 1)
            ve.reciprocal(rs, rs).then_inc(y_inv, 1)
            ve.wait_ge(y_inv, 1)
            ve.wait_ge(y_scaled, START + 2 * KT)
            for t, n in Y_TOK:
                ve.tensor_scalar(y[0:n, t, :], y[0:n, t, :], rs[0:n, t:t + 1], None, ALU.mult).then_inc(y_done, 1)

        @block.tensor
        def _(pe):
            pe.sem_inc(y_turned, START)
            def spread_rms(j):
                t, n = TOK[j]
                pe.wait_ge(diag_done, j + 1)
                out = psum[:, 7, t * P:(t + 1) * P] if t < TT else psum[:, 6, KT * NC:KT * NC + B]
                pe.matmul(out, unit_row[0:n, :], diag[t][0:n, 0:n], start=True, stop=True).then_inc(rms_spread, 1)

            pe.wait_ge(ident_set, 2)
            pe.wait_ge(unit_set, 1)
            for j, (t, n) in enumerate(TOK):
                pe.wait_ge(x_in[t], 16)
                if j >= 3:
                    pe.wait_ge(xT_done, j - 2)
                for k in range(KT):
                    last = pe.transpose(psum[:, 2 * (j % 3) + k // 4, (k % 4) * P:(k % 4) * P + n],
                                        x_tok[t][:, k * P:(k + 1) * P], ident[0:n, 0:n])
                last.then_inc(x_turned, 1)
                if j > 0:
                    spread_rms(j - 1)
                if j == TT - 1:
                    pe.wait_ge(rows_in, 16 * 8)
                    for k in range(KT):
                        last = pe.transpose(psum[:, 6, k * NC:(k + 1) * NC], crow[:, k * P:(k + 1) * P], ident[0:NC, 0:NC])
                    last.then_inc(cst_turned, 1)
            spread_rms(TT)

            def hi_pass(s, rhs, a, j, k, start):
                for part in range(2):
                    for h in range(2):
                        pe.matmul(a[:, h, :], w_hi[:, s, j, :], rhs[:, 2 * k + part, h * H:(h + 1) * H],
                                  start=start and part == 0, stop=False)

            def lo_pass(s, rhs, a, j, k, stop):
                for h in range(2):
                    last = pe.matmul(a[:, h, :], w_lo[:, s, j, :], rhs[:, 2 * k, h * H:(h + 1) * H], start=False, stop=stop)
                return last

            def unit(g, s, rhs, t=None, dst=None, ks=range(KT), first=True, final=True, done=None,
                     midway=None):
                t = g if t is None else t
                dst = s if dst is None else dst
                if first:
                    pe.wait_ge(evicted, out_of(t - 2))
                pe.wait_ge(hi_done, g + 1)
                a = psum[:, 2 * (dst % 2):2 * (dst % 2) + 2, 0:H]
                end = len(ks) - 1
                for j, k in enumerate(ks):
                    if j == end:
                        pe.wait_ge(lo_done, g + 1)
                        for jj in range(end):
                            lo_pass(s, rhs, a, jj, ks[jj], False)
                        if midway is not None:
                            midway()
                    if done is not None:
                        pe.wait_ge(*done(k))
                    hi_pass(s, rhs, a, j, k, first and j == 0)
                lo_pass(s, rhs, a, end, ks[end], final).then_inc(mm_done, 1)

            def first_units():
                a = [psum[:, 2 * s:2 * s + 2, 0:H] for s in range(2)]
                pe.wait_ge(rms_copied, 2)
                pe.wait_ge(xT_done, TT + 1)
                for k in range(KT):
                    pe.wait_ge((h_lo_even, h_lo_odd)[k % 2], k // 2 + 1)
                    for s in range(2):
                        if k == 0:
                            pe.wait_ge(hi_done, s + 1)
                        hi_pass(s, act, a[s], k, k, k == 0)
                for s in range(2):
                    pe.wait_ge(lo_done, s + 1)
                    for k in range(KT):
                        last = lo_pass(s, act, a[s], k, k, k == KT - 1)
                    last.then_inc(mm_done, 1)

            def mean_over_features(src):
                for h in range(2):
                    last = pe.matmul(psum[:, 6 + h, 0:H], ones, src[:, h * H:(h + 1) * H], start=True, stop=True)
                return last

            def tiles_from(a):
                return lambda k: (act_lo, START + a + 1 + k)

            first_units()
            for s in range(2, 8):
                unit(G_MIX + s, s % RING, act)
            with pe.Fori(1, KT // 2) as it:
                for s in range(8):
                    unit(G_MIX + 8 * it + s, s % RING, act)

            def b_unit(i, s):
                unit(G_B + i, s, act)
                pe.wait_ge(state_in[i % 2], 16 * (i // 2) + 16)
                pe.wait_ge(win_done, START + 2 * i)
                for h in range(2):
                    last = pe.transpose(psum[:, 4, h * SH:(h + 1) * SH], st_row[i % 2][:, h, :], ident[0:SH, 0:SH])
                last.then_inc(state_turned, 1)

            for s in range(RING):
                b_unit(s, s)
            pe.wait_ge(a_packed, 2)
            pe.wait_ge(tail_b_done, START + KT)
            for j, src in enumerate((a_pack[:, 0:SH], a_pack[:, SH:2 * SH], a_pack[:, 2 * SH:],
                                     tail_b[:, :, :].rearrange("p r t -> p (r t)"))):
                pe.transpose(psum[0:src.shape[1], 5, j * P:(j + 1) * P], src, ident[:, :]).then_inc(a_turned, 1)
            for s in range(RING):
                b_unit(RING + s, s)

            with pe.Fori(0, KT // RING) as it:
                for s in range(RING):
                    i = RING * it + s
                    unit(G_BOUT + i, s, mid, done=tiles_from(S_Q))

            def mean():
                pe.wait_ge(vsum_done, START + KT)
                pe.wait_ge(sum_zero, 3)
                mean_over_features(vsum).then_inc(mean_done, 1)

            def variance():
                pe.wait_ge(ssum_done, START + KT)
                pe.wait_ge(centred, KT)
                mean_over_features(ssum).then_inc(var_done, 1)

            for step in range(KT):
                unit(G_GATE + step, step % RING, act, midway={min(SQUARE_STEPS): mean, ROOT_STEP: variance}.get(step))
                if step == min(SQUARE_STEPS) + 1:
                    pe.wait_ge(frows_in, 32)
                    pe.wait_ge(win_done, START + 2 * KT)
                    for k in range(FT):
                        last = pe.transpose(psum[:, 4, k * NCF:(k + 1) * NCF], frow[:, k * P:(k + 1) * P], ident[0:NCF, 0:NCF])
                    last.then_inc(frow_turned, 1)
            with pe.Fori(KT // RING, 2 * KT // RING) as it:
                for s in range(RING):
                    unit(G_GATE + RING * it + s, s, act)

            for first, rhs, a in ((G_AOUT, mid, S_V), (G_O, act, S_M)):
                with pe.Fori(0, KT // RING) as it:
                    for s in range(RING):
                        unit(first + RING * it + s, s, rhs, done=tiles_from(a))

            def mean_square():
                pe.wait_ge(ssum_done, START + 2 * KT)
                mean_over_features(ssum).then_inc(var_done, 1)

            for s in range(RING):
                unit(G_UP + s, s, mid, done=tiles_from(S_H), midway=mean_square if s == 0 else None)
            with pe.Fori(1, FT // 2) as it:
                for s in range(RING):
                    unit(G_UP + RING * it + s, s, mid)

            pe.wait_ge(fg_tail, START + FT)
            pe.wait_ge(cst_f_done, 1)
            nf, hb = PADB * FT, B // 2 * FT
            tail = cst[:, :, :].rearrange("p t c -> p (t c)")
            for j, (c, n) in enumerate(((0, nf), (nf, hb), (nf + hb, hb))):
                if j == 2:
                    pe.wait_ge(var_eps, 2)
                pe.transpose(psum[0:n, 4 + j, 0:P], tail[:, c:c + n], ident[:, :]).then_inc(f_turned, 1)

            def turn(n, par):
                pe.wait_ge(evicted, out_of(G_DOWN + n))
                src = (t0, t1)[par]
                for t in range(TT):
                    pe.transpose(psum[:, 4 + 2 * par, t * P:(t + 1) * P], src[:, t * P:(t + 1) * P], ident[:, :])
                pe.transpose(psum[0:B, 5 + 2 * par, 0:P], src[:, SEQ:N], ident[:, :]).then_inc(y_turned, 1)

            def down(n, par, turned=None):
                for s in range(RING):
                    unit(G_DOWN + RING * n + s, s, act, t=G_DOWN + n, dst=par,
                         ks=range(KFIRST[s], KFIRST[s] + KSPLIT[s]), first=s == 0, final=s == RING - 1,
                         done=tiles_from(S_G))
                    if s == 0 and turned is not None:
                        turn(turned, 1 - par)

            down(0, 0)
            pe.wait_ge(f_staged, 3)
            with pe.Fori(0, KT // 2 - 1) as it:
                for par in range(2):
                    pe.wait_ge(y_scaled, START + 4 * it)
                    pe.wait_ge(y_squared, START + 2 * (TT + 1) * it)
                    down(2 * it + 1 + par, 1 - par, 2 * it + par)
            pe.wait_ge(y_scaled, START + 2 * (KT - 3))
            pe.wait_ge(y_squared, START + (TT + 1) * (KT - 3))
            down(KT - 1, 1, KT - 2)
            pe.wait_ge(y_scaled, START + 2 * (KT - 2))
            pe.wait_ge(y_squared, START + (TT + 1) * (KT - 2))
            turn(KT - 1, 1)


_INS = ['x_prompt', 'x_sample', 'state_conv_a', 'state_conv_b', 'state_conv_ffn', 'g_mix', 'w_in', 'conv_a_w',
        'conv_a_b', 'ln_a_g', 'ln_a_b', 'w_a_out', 'conv_b_w', 'w_b_out', 'w_o', 'g_ffn', 'w_up', 'conv_f_w',
        'w_down', 'g_final']


def kernel(**inputs):
    import numpy as np
    import concourse.bacc as bacc
    from concourse import mybir as mb
    from concourse.bass_utils import run_bass_kernel_spmd

    nc = bacc.Bacc("TRN2", target_bir_lowering=False, num_devices=1)
    arrays, args = {}, []
    for name in _INS:
        a = np.ascontiguousarray(inputs[name])
        arrays[f"in_{name}"] = a
        args.append(nc.dram_tensor(f"in_{name}", a.shape, mb.dt.from_np(a.dtype), kind="ExternalInput").ap())
    batch, seq, d = inputs["x_prompt"].shape
    depth, dec, pad_a, d_a = inputs["state_conv_a"].shape
    _, _, pad_b, d_b = inputs["state_conv_b"].shape
    _, _, pad_f, d_ff = inputs["state_conv_ffn"].shape
    outs = [(batch, seq, d), tuple(inputs["x_sample"].shape), (depth, batch, pad_a, d_a), (depth, batch, pad_b, d_b),
            (depth, batch, pad_f, d_ff), (depth, dec, pad_a, d_a), (depth, dec, pad_b, d_b), (depth, dec, pad_f, d_ff)]
    for i, shape in enumerate(outs):
        args.append(nc.dram_tensor(f"out_{i}", shape, mb.dt.float32, kind="ExternalOutput").ap())
    build(nc, *args)
    r = run_bass_kernel_spmd(nc, [arrays], core_ids=[0])
    return tuple(r.results[0][f"out_{i}"] for i in range(len(outs)))
```
